# Optimizing a Trainium2 kernel written in Bass

```python
import math
import jax, jax.numpy as jnp
from jax import lax
import numpy as np

D_MODEL = 1024
BATCH = 1
SEQ = 1024
DEPTH = 2

N_MEM = 256
HEAD_DIM = 64
N_MEM_HEADS = 4
MEM_W = N_MEM_HEADS * HEAD_DIM
MAIN_W = D_MODEL - MEM_W
MIX_W = MAIN_W + MEM_W
POOL_WINDOWS = (2, 4, 8, 16)
POOL_GROUP = MAIN_W // len(POOL_WINDOWS)
DIL_PATTERNS = ((128, 1), (512, 4), (2048, 16))
N_GROUPS = len(DIL_PATTERNS)
HEADS_PER_GROUP = MAIN_W // (N_GROUPS * HEAD_DIM)
N_DIL_HEADS = N_GROUPS * HEADS_PER_GROUP
N_A_LAYERS = DEPTH // 2
N_B_LAYERS = DEPTH - N_A_LAYERS
D_FF = ((8 * D_MODEL + 3 * 256 - 1) // (3 * 256)) * 256
ROPE_THETA = 10000.0
EPS = 1e-6
NEG = -1e30

kernel_name = "yoco_pool_dilated_hybrid"

def rms_norm(x, g):
    xf = x.astype(jnp.float32)
    y = xf * lax.rsqrt(jnp.mean(xf * xf, axis=-1, keepdims=True) + EPS)
    return (y * g.astype(jnp.float32)).astype(x.dtype)

def rope(t, positions):
    half = HEAD_DIM // 2
    freqs = ROPE_THETA ** (-jnp.arange(half, dtype=jnp.float32) / half)
    ang = positions.astype(jnp.float32)[..., None] * freqs
    cos = jnp.cos(ang)[:, :, None, :]
    sin = jnp.sin(ang)[:, :, None, :]
    tf = t.astype(jnp.float32)
    t1, t2 = tf[..., :half], tf[..., half:]
    return jnp.concatenate([t1 * cos - t2 * sin, t1 * sin + t2 * cos], axis=-1).astype(t.dtype)

def pool_mixer(u, w_pool, scale):
    S = u.shape[1]
    uf = u.astype(jnp.float32)
    c = jnp.cumsum(uf, axis=1)
    t = jnp.arange(S)
    outs = []
    for gi, w in enumerate(POOL_WINDOWS):
        sl = slice(gi * POOL_GROUP, (gi + 1) * POOL_GROUP)
        cg = c[..., sl]
        shifted = jnp.pad(cg, ((0, 0), (w, 0), (0, 0)))[:, :S]
        cnt = jnp.minimum(t + 1, w).astype(jnp.float32)[None, :, None]
        outs.append((cg - shifted) / cnt - uf[..., sl])
    p = jnp.stack(outs, axis=2).astype(u.dtype)
    y = jnp.einsum('bsgc,gce->bsge', p, w_pool).reshape(u.shape)
    return y * scale

def to_strided(t, d):
    B, S = t.shape[:2]
    return t.reshape((B, S // d, d) + t.shape[2:]).swapaxes(1, 2)

def kv_blocks(t, d, steps):
    s = to_strided(t, d)
    B, _, L, H, hd = s.shape
    nb = -(-L // steps)
    Lp = nb * steps
    s = jnp.pad(s, ((0, 0), (0, 0), (steps, Lp - L), (0, 0), (0, 0)))
    s = s.reshape(B, d, nb + 1, steps, H, hd)
    return jnp.concatenate([s[:, :, :-1], s[:, :, 1:]], axis=3)

def band_mask(nb, steps):
    i = jnp.arange(steps)[:, None] + steps
    j = jnp.arange(2 * steps)[None, :]
    rel = i - j
    m = (rel >= 0) & (rel <= steps)
    n = jnp.arange(nb)[:, None, None]
    return m[None] & ((n > 0) | (j >= steps)[None])

def dilated_group_attn(q, kk, vv, d, steps):
    B, S, H, hd = q.shape
    L = S // d
    nb = kk.shape[2]
    Lp = nb * steps
    qs = jnp.pad(to_strided(q, d), ((0, 0), (0, 0), (0, Lp - L), (0, 0), (0, 0)))
    qs = qs.reshape(B, d, nb, steps, H, hd)
    s = jnp.einsum('bdnqhe,bdnkhe->bdnhqk', qs, kk).astype(jnp.float32) * (HEAD_DIM ** -0.5)
    s = jnp.where(band_mask(nb, steps)[None, None, :, None], s, NEG)
    lse = jax.nn.logsumexp(s, axis=-1)
    p = jnp.exp(s - lse[..., None]).astype(vv.dtype)
    o = jnp.einsum('bdnhqk,bdnkhe->bdnqhe', p, vv)
    o = o.reshape(B, d, Lp, H, hd)[:, :, :L].swapaxes(1, 2).reshape(B, S, H, hd)
    lse = lse.transpose(0, 1, 2, 4, 3).reshape(B, d, Lp, H)[:, :, :L].swapaxes(1, 2).reshape(B, S, H)
    return o, lse

def build_shared_kv(x, positions, kv_norm, w_kv):
    B, S, _ = x.shape
    kv = rms_norm(x, kv_norm) @ w_kv
    k = rope(kv[..., :MAIN_W].reshape(B, S, N_DIL_HEADS, HEAD_DIM), positions)
    v = kv[..., MAIN_W:].reshape(B, S, N_DIL_HEADS, HEAD_DIM)
    k = k.reshape(B, S, N_GROUPS, HEADS_PER_GROUP, HEAD_DIM)
    v = v.reshape(B, S, N_GROUPS, HEADS_PER_GROUP, HEAD_DIM)
    shared = []
    for g, (win, d) in enumerate(DIL_PATTERNS):
        steps = win // d
        shared.append((kv_blocks(k[:, :, g], d, steps), kv_blocks(v[:, :, g], d, steps)))
    return shared

def dilated_mixer(zq, positions, shared):
    B, S, _ = zq.shape
    q = rope(zq.reshape(B, S, N_DIL_HEADS, HEAD_DIM), positions)
    q = q.reshape(B, S, N_GROUPS, HEADS_PER_GROUP, HEAD_DIM)
    outs, lses = [], []
    for g, (win, d) in enumerate(DIL_PATTERNS):
        kk, vv = shared[g]
        o, l = dilated_group_attn(q[:, :, g], kk, vv, d, win // d)
        outs.append(o)
        lses.append(l)
    o = jnp.stack(outs, axis=2)
    alpha = jax.nn.softmax(jnp.stack(lses, axis=2), axis=2)
    return (o * alpha[..., None].astype(o.dtype)).reshape(B, S, MAIN_W)

def memory_attn(zm, mem, g, w_mkv):
    B, S, _ = zm.shape
    M = mem.shape[1]
    q = zm.reshape(B, S, N_MEM_HEADS, HEAD_DIM)
    kv = rms_norm(mem, g) @ w_mkv
    km = kv[..., :MEM_W].reshape(B, M, N_MEM_HEADS, HEAD_DIM)
    vm = kv[..., MEM_W:].reshape(B, M, N_MEM_HEADS, HEAD_DIM)
    s = jnp.einsum('bshe,bmhe->bhsm', q, km).astype(jnp.float32) * (HEAD_DIM ** -0.5)
    p = jax.nn.softmax(s, axis=-1).astype(vm.dtype)
    return jnp.einsum('bhsm,bmhe->bshe', p, vm).reshape(B, S, MEM_W)

def setup_inputs(seed: int = 0) -> dict:
    key = jax.random.key(seed)
    ks = jax.random.split(key, 14)
    f32 = jnp.float32
    nrm = lambda k, shape, fan: jax.random.normal(k, shape, f32) * (fan ** -0.5)
    return {
        "x": jax.random.normal(ks[0], (BATCH, SEQ, D_MODEL), f32),
        "mem": jax.random.normal(ks[1], (BATCH, N_MEM, D_MODEL), f32),
        "positions": jnp.broadcast_to(jnp.arange(SEQ, dtype=jnp.int32)[None], (BATCH, SEQ)),
        "norm_gains": 1.0 + 0.05 * jax.random.normal(ks[2], (DEPTH, 4, D_MODEL), f32),
        "mem_norm": 1.0 + 0.05 * jax.random.normal(ks[3], (DEPTH, D_MODEL), f32),
        "w_in": nrm(ks[4], (DEPTH, D_MODEL, MIX_W), D_MODEL),
        "w_mem_kv": nrm(ks[5], (DEPTH, D_MODEL, 2 * MEM_W), D_MODEL),
        "w_out": nrm(ks[6], (DEPTH, MIX_W, D_MODEL), MIX_W),
        "w_pool": nrm(ks[7], (N_A_LAYERS, len(POOL_WINDOWS), POOL_GROUP, POOL_GROUP), POOL_GROUP),
        "pool_scale": 1.0 + 0.1 * jax.random.normal(ks[8], (N_A_LAYERS, MAIN_W), f32),
        "kv_norm": 1.0 + 0.05 * jax.random.normal(ks[9], (D_MODEL,), f32),
        "w_kv": nrm(ks[10], (D_MODEL, 2 * MAIN_W), D_MODEL),
        "w_gate_up": nrm(ks[11], (DEPTH, D_MODEL, 2 * D_FF), D_MODEL),
        "w_down": nrm(ks[12], (DEPTH, D_FF, D_MODEL), D_FF),
    }

def reference(x, mem, positions, norm_gains, mem_norm, w_in, w_mem_kv, w_out,
              w_pool, pool_scale, kv_norm, w_kv, w_gate_up, w_down):
    shared = None
    for l in range(DEPTH):
        h = rms_norm(x, norm_gains[l, 0])
        z = h @ w_in[l]
        z_main, z_mem = z[..., :MAIN_W], z[..., MAIN_W:]
        if l < N_A_LAYERS:
            y_main = pool_mixer(z_main, w_pool[l], pool_scale[l])
        else:
            y_main = dilated_mixer(z_main, positions, shared)
        y_mem = memory_attn(z_mem, mem, mem_norm[l], w_mem_kv[l])
        y = jnp.concatenate([y_main, y_mem], axis=-1) @ w_out[l]
        x = x + rms_norm(y, norm_gains[l, 1])
        h = rms_norm(x, norm_gains[l, 2])
        gu = h @ w_gate_up[l]
        y = (jax.nn.silu(gu[..., :D_FF]) * gu[..., D_FF:]) @ w_down[l]
        x = x + rms_norm(y, norm_gains[l, 3])
        if l == N_A_LAYERS - 1:
            shared = build_shared_kv(x, positions, kv_norm, w_kv)
    return x


_drawn_inputs = setup_inputs


def setup_inputs(seed=0):
    import zlib

    import numpy as np

    out = dict(_drawn_inputs(seed))
    spreads = {}
    factors = {}
    for name, (base, spread) in spreads.items():
        noise = np.random.default_rng([zlib.crc32(name.encode()), seed]).standard_normal(out[name].shape)
        drawn = base * np.exp(spread * noise) if base else spread * noise
        out[name] = __import__('jax').numpy.asarray(drawn.astype(out[name].dtype))
    for name, factor in factors.items():
        out[name] = (out[name] * factor).astype(out[name].dtype)
    return out
```

```python
from contextlib import ExitStack

import numpy as np

import concourse.bass as bass
from concourse import mybir

F32 = mybir.dt.float32
F32R = mybir.dt.float32r
I32 = mybir.dt.int32
ALU = mybir.AluOpType
ACT = mybir.ActivationFunctionType
AX_X = mybir.AxisListType.X

P = 128
D = 1024
S = 1024
KT = D // P
HB = S // 2
MEM = 256
DH = 64
MAIN = 768
NMT = MAIN // P
DFF = 2816
NFT = DFF // P
CHUNKS = (8, 8, 6)
WINDOWS = (2, 4, 8, 16)
POOLG = MAIN // 4
DIL = (1, 4, 16)
PAD = 16
EPS = 1e-6
SCALE = DH ** -0.5
NEG = -1e30
SUMROW = 1.5 * 2.0 ** 23

G_POOL = 8 * 11
NGAIN = G_POOL + NMT
C_ID = 0
C_ONE = C_ID + P
C_EDGE = C_ONE + P
C_INVW = C_EDGE + NMT * PAD
C_FREQ = C_INVW + NMT
C_SIGN = C_FREQ + 1
C_EPS = C_SIGN + 1
C_HPI = C_EPS + 1
NCONST = C_HPI + 1


def as_f32(ap):
    return ap.bitcast(F32)


def plan_units():
    units = []
    for l in range(2):
        units += [("mem", l, m, KT, 8 + l) for m in range(4)]
        if l == 1:
            units += [("kv", l, m, KT, 10) for m in range(2 * NMT)]
        units += [("in", l, m, KT, 4 * l) for m in range(KT)]
        if l == 0:
            units += [("pool", l, m, 3, None) for m in range(NMT)]
        units += [("out", l, m, KT, None) for m in range(KT)]
        f0 = 0
        for c, n in enumerate(CHUNKS):
            for f in range(f0, f0 + n):
                units += [("ffn", l, (c, f, 0), KT, 4 * l + 2), ("ffn", l, (c, f, 1), KT, 4 * l + 2)]
            units += [("down", l, (c, m), n, None) for m in range(KT)]
            f0 += n
    return units


UNITS = plan_units()
NU = len(UNITS)


def first_unit(name, layer, chunk=None):
    for u, (nm, l, i, _, _) in enumerate(UNITS):
        if nm == name and l == layer and (chunk is None or i[0] == chunk):
            return u
    raise ValueError(name)


def runs_of_units():
    runs = []
    for u, (nm, l, _, k, g) in enumerate(UNITS):
        if runs and runs[-1][2:] == [k, g, (nm, l)]:
            runs[-1][1] += 1
        else:
            runs.append([u, 1, k, g, (nm, l)])
    return runs


RUNS = runs_of_units()
U_OUT1 = first_unit("out", 1)


def build(nc, w_all, x_t, mem_t, pos, gains, consts, masks, k_scr, v_scr, out_t):
    with ExitStack() as ctx:
        base = nc.sbuf_base + (-nc.sbuf_base) % 64
        cursor = [base]
        fence = ctx.enter_context(nc.sbuf_tensor("fence", [P, 222 * 256], F32))
        del fence

        def at(name, shape, dt, offset):
            return nc.alloc_sbuf_tensor_at(name, shape, dt, offset=offset)

        def take(nbytes):
            o = cursor[0]
            cursor[0] += nbytes + -nbytes % 32
            assert cursor[0] - base <= 222 * 1024
            return o

        def sem(name):
            return ctx.enter_context(nc.semaphore(name))

        TILE = 4 * S
        XH = at("XH", [P, KT, S], F32R, take(KT * TILE))
        XL = at("XL", [P, KT, S], F32R, take(KT * TILE))
        CH = at("CH", [P, KT, S], F32R, take(KT * TILE))
        CL = at("CL", [P, KT, S], F32R, take(KT * TILE))
        o_y = take(KT * TILE)
        Y = at("Y", [P, KT, S], F32, o_y)
        o_w = take(6 * TILE)
        WR = at("WR", [P, 2, KT, P], F32, o_w)
        WH = at("WH", [P, 2, KT, P], F32R, o_w + 2 * TILE)
        WL = at("WL", [P, 2, KT, P], F32R, o_w + 4 * TILE)
        RSTD = at("RSTD", [P, S], F32, take(TILE))
        SS = at("SS", [P, S], F32, take(TILE))
        o_t = [take(4 * (S + PAD)) for _ in range(4)]
        TP = [at(f"TP{i}", [P, S + PAD], F32, o_t[i]) for i in range(4)]
        T = [t[:, PAD:PAD + S] for t in TP]
        MR = at("MR", [P, KT, MEM], F32, o_t[0])
        MS = at("MS", [P, KT, MEM], F32, o_t[2])
        KM = [at(f"KM{i}", [P, 2, MEM], F32R, take(8 * MEM)) for i in range(2)]
        VM = [at(f"VM{i}", [P, 2, 2, 192], F32R, take(16 * 192)) for i in range(2)]
        RSTDM = at("RSTDM", [P, MEM], F32, take(4 * MEM))
        GN = at("GN", [P, NGAIN], F32, take(4 * NGAIN))
        CN = at("CN", [P, NCONST], F32, take(4 * NCONST))
        MC = at("MC", [P, 2, 8], F32, take(64))
        NM = at("NM", [P, 2], F32, take(8))
        COS = at("COS", [P, S], F32, o_y)
        SIN = at("SIN", [P, S], F32, o_y + TILE)
        POS = at("POS", [P, S], I32, o_y + TILE)
        STG = [at(f"STG{i}", [P, S], F32R, o_y + (2 + i) * TILE) for i in range(2)]
        VA = [at(f"VA{i}", [P, 8, 192], F32R, o_y + i * 8 * 192 * 4) for i in range(2)]
        KA = [at(f"KA{i}", [P, S], F32R, o_y + (3 + i) * TILE) for i in range(2)]
        MK = at("MK", [P, 3 * P], F32, o_y + 5 * TILE)
        SM = at("SM", [P, 2, 256], F32, o_y + 6 * TILE)
        PR = at("PR", [P, 2, 256], F32, o_y + 6 * TILE + 2048)
        PT = [at(f"PT{i}", [P, 2, 256], F32R, o_y + 7 * TILE + 2048 * i) for i in range(2)]
        OB = [at(f"OB{g}", [P, S], F32, o_w + g * TILE) for g in range(3)]
        LB = [at(f"LB{g}", [P, S], F32, o_w + (3 + g) * TILE) for g in range(3)]
        MB = [T[g] for g in range(3)]

        IDENT = CN[:, C_ID:C_ID + P]
        ONES = CN[:, C_ONE:C_ONE + P]

        PS = [ctx.enter_context(nc.psum_tensor(f"PS{i}", [P, S], F32)) for i in range(2)]
        PV2 = ctx.enter_context(nc.psum_tensor("PV2", [P, S], F32))
        PN = ctx.enter_context(nc.psum_tensor("PN", [P, S], F32))
        PSC = [PS[0][:, 0:256], PS[0][:, HB:HB + 256]]
        PTR = [PS[1][:, 0:256], PS[1][:, HB:HB + 256]]
        PO = [PV2[:, 0:HB], PV2[:, HB:S]]

        w_loaded = [sem(f"w_loaded{i}") for i in range(2)]
        w_gained = sem("w_gained")
        w_hi = sem("w_hi")
        w_lo = sem("w_lo")
        mm_done = sem("mm_done")
        consts_in = sem("consts_in")
        x_in = sem("x_in")
        mem_in = sem("mem_in")
        pos_in = sem("pos_in")
        mask_in = sem("mask_in")
        kv_in = sem("kv_in")
        spilled = sem("spilled")
        out_done = sem("out_done")
        mem_sq = sem("mem_sq")
        mem_hi = sem("mem_hi")
        mem_ss = sem("mem_ss")
        mem_lo = sem("mem_lo")
        mem_scaled = sem("mem_scaled")
        km_hi = sem("km_hi")
        km_lo = sem("km_lo")
        vm_tr = sem("vm_tr")
        vm_hi = sem("vm_hi")
        vm_lo = sem("vm_lo")
        ones_set = sem("ones_set")
        norm_sum = sem("norm_sum")
        norm_root = sem("norm_root")
        norm_done = sem("norm_done")
        sq_done = sem("sq_done")
        ss_done = sem("ss_done")
        y_first = sem("y_first")
        x_sum = sem("x_sum")
        res_done = sem("res_done")
        x_hi = sem("x_hi")
        x_lo = sem("x_lo")
        pads_zero = sem("pads_zero")
        in_scaled = sem("in_scaled")
        pooled = sem("pooled")
        mix_ready = sem("mix_ready")
        c_hi = sem("c_hi")
        c_lo = sem("c_lo")
        ypool_done = sem("ypool_done")
        silu_in = sem("silu_in")
        up_scaled = sem("up_scaled")
        silu_done = sem("silu_done")
        prod_done = sem("prod_done")
        a_hi = sem("a_hi")
        a_lo = sem("a_lo")
        y_part = sem("y_part")
        ang_ready = sem("ang_ready")
        trig_done = sem("trig_done")
        cos_part = sem("cos_part")
        swapped = sem("swapped")
        roped = sem("roped")
        v_scaled = sem("v_scaled")
        v_tr = sem("v_tr")
        st_hi = sem("st_hi")
        st_lo = sem("st_lo")
        scored = sem("scored")
        max_done = sem("max_done")
        exp_done = sem("exp_done")
        p_tr = sem("p_tr")
        pt_hi = sem("pt_hi")
        pt_lo = sem("pt_lo")
        pv_done = sem("pv_done")
        o_free = sem("o_free")
        mb_cast = sem("mb_cast")
        mb_tr = sem("mb_tr")
        mb_out = sem("mb_out")
        mdiff = sem("mdiff")
        mexp = sem("mexp")
        dve_own = sem("dve_own")
        pool_own = sem("pool_own")

        U_MEM = [first_unit("mem", l) for l in range(2)]
        U_IN = [first_unit("in", l) for l in range(2)]
        U_OUT = [first_unit("out", l) for l in range(2)]
        U_KV = first_unit("kv", 1)
        U_POOL = first_unit("pool", 0)
        U_FFN = [[first_unit("ffn", l, c) for c in range(3)] for l in range(2)]
        U_DOWN = [[first_unit("down", l, c) for c in range(3)] for l in range(2)]

        def released(u):
            name, l, i, _, _ = UNITS[u]
            if name == "mem":
                return mem_scaled, 4 * l + i + 1
            if name == "kv":
                return (swapped, 4 * (i + 1)) if i < NMT else (v_scaled, i - NMT + 1)
            if name == "in":
                if i >= NMT:
                    return mix_ready, 8 * l + i + 1
                return (swapped, 4 * (NMT + i + 1)) if l else (in_scaled, i + 1)
            if name == "pool":
                return ypool_done, i + 1
            if name == "out":
                return y_first, 16 * l + i + 1
            if name == "ffn":
                return (up_scaled if i[2] else silu_in), 22 * l + i[1] + 1
            c, m = i
            return (y_first, 16 * l + 8 + m + 1) if c == 0 else (y_part, 16 * l + 8 * (c - 1) + m + 1)

        def outputs_out(o):
            return o + 1 if o < 16 else 16 + 2 * (o - 15)

        def lag(eng, s, value, back):
            if value - back > 0:
                eng.wait_ge(s, value - back)

        N_MEM = (0, 6)
        N_X = (1, 3, 5, 8)
        N_Y = (2, 4, 7, 9)
        SERIES_OF = {1: 0, 2: 1, 3: 2, 4: 3, 5: 4, 7: 5, 8: 6, 9: 7}

        SLOTS = [("mem", 0, 6), ("mem", 0, 7), ("mem", 1, 6), ("mem", 1, 7)]
        SLOTS += [("dil", 1, 2 * g + pair) for pair in range(2) for g in range(3)]

        def key_span(sl, n):
            kind, _, t = SLOTS[sl]
            if kind == "mem":
                return 0, MEM, None
            g = t // 2
            if g == 2:
                return P * n, P, (2 * P, 3 * P)
            if (g == 0 and n == 0) or (g == 1 and n % 2 == 0):
                return P * n, P, (P, 2 * P)
            return P * (n - 1), 2 * P, (0, 2 * P)

        def sorted_cols(ap, g):
            d = DIL[g]
            return ap.rearrange("p (l r) -> p r l", r=d)

        block = ctx.enter_context(nc.Block())

        @block.sync
        def _(sp):
            sp.dma_start(CN[:, :], consts).then_inc(consts_in, 16)
            sp.dma_start(GN[:, :], gains).then_inc(consts_in, 16)

            def load_mem(l):
                if l:
                    sp.wait_ge(res_done, 16)
                sp.dma_start(MR[:, :, :], mem_t).then_inc(mem_in, 16)

            def load_unit(u, slot, k):
                lag(sp, w_lo, u + 1, 2) if isinstance(u, int) else sp.wait_ge(w_lo, u - 1)
                sp.dma_start(WR[:, slot, 0:k, :],
                             w_all[bass.ds(u, 1), :, 0:k * P].rearrange("a p (k n) -> (a p) k n", k=k)
                             ).then_inc(w_loaded[slot], 16)

            def load_run(u0, n, k):
                if u0 == 0 or n <= 4:
                    for u in range(u0, u0 + n):
                        load_unit(u, u % 2, k)
                    return
                with sp.Fori(0, n // 2) as it:
                    for j in range(2):
                        load_unit(u0 + j + 2 * it, j, k)

            load_mem(0)
            for k in range(KT):
                sp.dma_start(Y[:, k, :], x_t[:, k, :]).then_inc(x_in, 16)
            for u0, n, k, _, (name, l) in RUNS:
                if name == "mem" and l == 1:
                    for u in range(u0, u0 + 2):
                        load_unit(u, u % 2, k)
                    load_mem(1)
                    sp.wait_ge(x_lo, 24)
                    sp.wait_ge(sq_done, 8 * 5)
                    sp.dma_start(POS[:, :], pos.to_broadcast([P, S])).then_inc(pos_in, 16)
                    load_run(u0 + 2, 2, k)
                    continue
                if name == "kv":
                    for m in range(2 * NMT):
                        load_unit(u0 + m, m % 2, k)
                        if m >= 2:
                            sp.wait_ge(st_lo, m - 1)
                            dst = (k_scr if m - 2 < NMT else v_scr)[(m - 2) % NMT]
                            for i in range(2):
                                sp.dma_start(dst[i], STG[i][:, :].bitcast(F32)).then_inc(spilled, 16)
                    continue
                if name == "in" and l == 1:
                    for m in range(2 * NMT - 2, 2 * NMT):
                        load_unit(u0 + m - (2 * NMT - 2), m % 2, k)
                        sp.wait_ge(st_lo, m + 1)
                        dst = v_scr[m % NMT]
                        for i in range(2):
                            sp.dma_start(dst[i], STG[i][:, :].bitcast(F32)).then_inc(spilled, 16)
                    load_run(u0 + 2, n - 2, k)
                    sp.wait_ge(c_lo, 24)
                    sp.wait_ge(spilled, 16 * 2 * 2 * NMT)
                    sp.dma_start(MK[:, :], masks).then_inc(mask_in, 16)
                    for i in range(6):
                        t = SLOTS[4 + i][2]
                        if i:
                            sp.wait_ge(pv_done, 64 + 16 * i)
                        for part in range(2):
                            sp.dma_start(KA[part][:, :].bitcast(F32), k_scr[t, part]).then_inc(kv_in, 16)
                            if i == 0:
                                sp.wait_ge(ones_set, 3 + part)
                            va = VA[part][:, :, :].bitcast(F32).rearrange("p n (h c) -> p n h c", h=3)
                            vs = v_scr[t, part].rearrange("p (n h c) -> p n h c", n=8, h=2)
                            for h in range(2):
                                sp.dma_start(va[:, :, 2 * h, :], vs[:, :, h, :]).then_inc(kv_in, 16)
                    sp.wait_ge(c_lo, 32)
                    continue
                load_run(u0, n, k)
            for k in range(KT):
                sp.wait_ge(res_done, 8 * 3 + k + 1)
                sp.dma_start(out_t[:, k, :], Y[:, k, :]).then_inc(out_done, 16)
            sp.wait_ge(out_done, 16 * KT)

        @block.gpsimd
        def _(pool):
            own = [0]

            def link(ins):
                own[0] += 1
                ins.then_inc(pool_own, 1)
                pool.wait_ge(pool_own, own[0])

            def gain(u, slot, pairs, k, g):
                pool.wait_ge(w_loaded[slot], 16 * pairs)
                raw = WR[:, slot, 0:k, :]
                col = GN[:, 8 * g:8 * g + k] if g is not None else CN[:, C_ONE:C_ONE + k]
                nc.gpsimd.tensor_tensor(raw, raw, col.unsqueeze(2).to_broadcast([P, k, P]),
                                        ALU.mult).then_inc(w_gained, 1)

            def accumulate(s, k):
                pool.wait_ge(sq_done, 8 * s + k + 1)
                src = T[2 + k % 2]
                if k == 0:
                    if s == 0:
                        pool.wait_ge(norm_sum, 1)
                    else:
                        pool.wait_ge(norm_sum, [n for n in SERIES_OF if SERIES_OF[n] == s][0])
                    nc.gpsimd.tensor_copy(SS[:, :], src).then_inc(ss_done, 1)
                else:
                    pool.wait_ge(ss_done, 8 * s + k)
                    nc.gpsimd.tensor_tensor(SS[:, :], SS[:, :], src, ALU.add).then_inc(ss_done, 1)

            def stream_sum(j, k):
                r = 8 * (j - 1) + k
                if j == 1 and k < 2:
                    pool.wait_ge(c_lo, 16)
                elif k >= 2:
                    pool.wait_ge(res_done, r - 1)
                elif j == 3:
                    pool.wait_ge(c_lo, 32)
                nc.gpsimd.tensor_tensor(T[k % 2], as_f32(XH[:, k, :]), as_f32(XL[:, k, :]), ALU.add).then_inc(x_sum, 1)

            def residual(j):
                if j in (2, 4):
                    pool.wait_ge(a_lo, 22 * (j // 2))
                stream_sum(j, 0)
                stream_sum(j, 1)
                for k in range(KT):
                    if j < 4:
                        accumulate(2 * j, k)
                    if k + 2 < KT:
                        stream_sum(j, k + 2)

            pool.wait_ge(consts_in, 32)
            for i, value in enumerate((1.0, 0.0)):
                nc.gpsimd.memset(as_f32(VM[i][:, :, :, DH:2 * DH]), value).then_inc(ones_set, 1)
            gained = [0]

            def gains_to(end):
                for u0, n, k, g, _ in RUNS:
                    a, b = max(u0, gained[0]), min(u0 + n, end)
                    if b - a >= 4 and a % 2 == 0:
                        pairs = (b - a) // 2
                        with pool.Fori(0, pairs) as it:
                            for j in range(2):
                                gain(a + j + 2 * it, j, it + (a // 2 + 1), k, g)
                        a += 2 * pairs
                    for u in range(a, b):
                        gain(u, u % 2, u // 2 + 1, k, g)
                gained[0] = max(gained[0], end)

            gains_to(2)
            for k in range(KT):
                accumulate(0, k)
            gains_to(U_IN[0] + 2)
            pool.wait_ge(mem_lo, 1)
            pool.wait_ge(vm_tr, 2)
            pool.wait_ge(km_lo, 2)
            for i in range(3):
                nc.gpsimd.memset(TP[i][:, 0:PAD], 0.0).then_inc(pads_zero, 1)
            pool.wait_ge(pads_zero, 3)
            for m in range(NMT):
                pool.wait_ge(in_scaled, m + 1)
                levels = []
                for w in WINDOWS:
                    rows = [r for r in range(P) if WINDOWS[(m * P + r) // POOLG] >= w]
                    if rows:
                        levels.append((w // 2, rows[0]))
                src = TP[0]
                for i, (shift, r0) in enumerate(levels):
                    dst = TP[1 + i % 2]
                    if r0:
                        link(nc.gpsimd.tensor_copy(dst[0:r0, PAD:], src[0:r0, PAD:]))
                    link(nc.gpsimd.tensor_tensor(dst[r0:P, PAD:], src[r0:P, PAD:],
                                                 src[r0:P, PAD - shift:PAD + S - shift], ALU.add))
                    src = dst
                edge = CN[:, C_EDGE + PAD * m:C_EDGE + PAD * (m + 1)]
                nc.gpsimd.tensor_tensor(src[:, PAD:2 * PAD], src[:, PAD:2 * PAD], edge,
                                        ALU.mult).then_inc(pooled, 1)
                gains_to(U_IN[0] + m + 3)
            for l in range(2):
                gains_to(U_OUT[l] + 2)
                for m in range(KT):
                    accumulate(4 * l + 1, m)
                    gains_to(U_OUT[l] + m + 3)
                residual(2 * l + 1)
                gains_to(U_DOWN[l][2] + 2)
                for m in range(KT):
                    accumulate(4 * l + 3, m)
                    gains_to(min(NU, U_DOWN[l][2] + m + 3))
                residual(2 * l + 2)
                if l == 0:
                    gains_to(U_OUT1)
                    pool.wait_ge(c_lo, 24)
                    pool.wait_ge(spilled, 16 * 4 * NMT)
                    for i, value in enumerate((1.0, 0.0)):
                        nc.gpsimd.memset(as_f32(VA[i][:, :, DH:2 * DH]), value).then_inc(ones_set, 1)
                    pool.wait_ge(c_lo, 32)

        @block.scalar
        def _(act):
            A = nc.scalar.activation

            def weight_hi(u, slot, k=KT):
                act.wait_ge(w_gained, u + 1)
                if not isinstance(u, int) or u >= 2:
                    act.wait_ge(mm_done, u - 1)
                A(WH[:, slot, 0:k, :], WR[:, slot, 0:k, :], ACT.Copy).then_inc(w_hi, 1)

            def ahead(u):
                v = u + 2
                if v < NU and v not in (U_OUT1, U_OUT1 + 1):
                    weight_hi(v, v % 2, UNITS[v][3])

            def root(n, width, dst):
                act.wait_ge(norm_sum, n + 1)
                A(dst[:, 0:width], PN[:, 0:width], ACT.Sqrt, scale=1.0 / D,
                  bias=CN[:, C_EPS:C_EPS + 1]).then_inc(norm_root, 1)

            def square(s, k, src):
                if 8 * s + k >= 2:
                    act.wait_ge(ss_done, 8 * s + k - 1)
                return A(T[2 + k % 2], src, ACT.Square).then_inc(sq_done, 1)

            def residual(j):
                for k in range(KT):
                    if j == 0:
                        act.wait_ge(x_in, 16 * KT)
                    else:
                        act.wait_ge(res_done, 8 * (j - 1) + k + 1)
                    A(XH[:, k, :], Y[:, k, :], ACT.Copy).then_inc(x_hi, 1)
                    square(2 * j, k, Y[:, k, :])

            def memory(l):
                act.wait_ge(mem_in, 16 * (l + 1))
                if l:
                    act.wait_ge(ss_done, 8 * 5)
                A(MS[:, :, :], MR[:, :, :], ACT.Square).then_inc(mem_sq, 1)
                if l:
                    act.wait_ge(mm_done, U_MEM[1])
                A(CH[:, 0:2, :].rearrange("p a (b t) -> p (a b) t", b=4), MR[:, :, :],
                  ACT.Copy).then_inc(mem_hi, 1)

            def memory_kv(l):
                root(N_MEM[l], MEM, RSTDM)
                for m in range(4):
                    act.wait_ge(mem_scaled, 4 * l + m + 1)
                    if m < 2:
                        if l:
                            act.wait_ge(scored, 32)
                        A(KM[0][:, m, :], TP[2][:, m * MEM:(m + 1) * MEM], ACT.Copy).then_inc(km_hi, 1)
                    ahead(U_MEM[l] + m)
                act.wait_ge(vm_tr, 2 * l + 2)
                if l:
                    act.wait_ge(pv_done, 32)
                for i in range(2):
                    A(VM[0][:, i, :, :].rearrange("p a (h c) -> p a h c", h=3)[:, :, 0:3:2, :],
                      PV2[:, 2 * P * i:2 * P * (i + 1)].rearrange("p (a h c) -> p a h c", a=2, h=2),
                      ACT.Copy).then_inc(vm_hi, 1)

            def tile_hi(n, dst, src):
                act.wait_ge(mix_ready, n + 1)
                A(dst, src, ACT.Copy).then_inc(c_hi, 1)

            def halves_swapped(u):
                for i in range(4):
                    r, q = 32 * i, 32 * (i ^ 1)
                    A(T[1][r:r + 32, :], PS[u % 2][q:q + 32, :], ACT.Copy).then_inc(swapped, 1)

            def attention(slots, n_before, evacuate):
                tiles = [(sl, h, n) for sl in slots for h in range(2) for n in range(8)]
                a0 = n_before
                for i in range(len(tiles) + 2):
                    if i < len(tiles):
                        a = a0 + i
                        sl, h, n = tiles[i]
                        _, nk, mask = key_span(sl, n)
                        act.wait_ge(max_done, a + 1)
                        lag(act, p_tr, a + 1, 2)
                        src = SM[:, a % 2, 0:nk] if mask else PSC[a % 2][:, 0:nk]
                        A(PR[:, a % 2, 0:nk], src, ACT.Exp, scale=SCALE,
                          bias=NM[:, a % 2:a % 2 + 1]).then_inc(exp_done, 1)
                    if 1 <= i <= len(tiles):
                        a = a0 + i - 1
                        nk = key_span(tiles[i - 1][0], tiles[i - 1][2])[1]
                        act.wait_ge(p_tr, a + 1)
                        lag(act, pv_done, a + 1, 2)
                        A(PT[0][:, a % 2, 0:nk], PTR[a % 2][:, 0:nk], ACT.Copy).then_inc(pt_hi, 1)
                    if i >= 2 and (i - 2) % 4 == 3:
                        evacuate(a0 + i - 2, *tiles[i - 2])

            act.wait_ge(consts_in, 32)
            memory(0)
            for u in range(2):
                weight_hi(u, u)
            act.wait_ge(mem_ss, 1)
            residual(0)
            memory_kv(0)
            root(N_X[0], S, RSTD)

            n_tile = 0
            for m in range(KT):
                u = U_IN[0] + m
                if m == 0:
                    act.wait_ge(vm_tr, 2)
                ahead(u)
                tile_hi(n_tile, CH[:, m, :], T[3])
                n_tile += 1
            for m in range(NMT):
                u = U_POOL + m
                act.wait_ge(mm_done, u + 1)
                if m == 0:
                    act.wait_ge(x_hi, 8)
                A(Y[:, m, :], PS[u % 2][:, :], ACT.Copy,
                  scale=GN[:, G_POOL + m:G_POOL + m + 1]).then_inc(ypool_done, 1)
                if m + 2 < NMT:
                    ahead(u)
            for u in (U_POOL + NMT - 2, U_POOL + NMT - 1):
                ahead(u)
            act.wait_ge(mm_done, U_POOL + NMT)
            for m in range(NMT):
                act.wait_ge(ypool_done, m + 1)
                A(CH[:, m, :], Y[:, m, :], ACT.Copy).then_inc(c_hi, 1)
                n_tile += 1
            attention([0, 1], 0, lambda *a: None)
            for m in range(2):
                act.wait_ge(o_free, 4 * (m + 1))
                A(CH[:, NMT + m, :], T[1] if m else T[0], ACT.Copy).then_inc(c_hi, 1)
                n_tile += 1

            def sub_layer(l):
                for m in range(KT):
                    u = U_OUT[l] + m
                    act.wait_ge(mm_done, u + 1)
                    if m == 0:
                        act.wait_ge(c_lo, 16 if l == 0 else 32)
                    square(4 * l + 1, m, PS[u % 2][:, :])
                    A(Y[:, m, :], PS[u % 2][:, :], ACT.Copy).then_inc(y_first, 1)
                    ahead(u)
                root(N_Y[2 * l], S, RSTD)
                residual(2 * l + 1)
                root(N_X[2 * l + 1], S, RSTD)
                for c, nf in enumerate(CHUNKS):
                    u0, f0 = U_FFN[l][c], 22 * l + 8 * c
                    with act.Fori(0, nf) as f:
                        weight_hi(u0 + 2 + 2 * f, 0)
                        act.wait_ge(silu_in, f + (f0 + 1))
                        A(T[1], T[0], ACT.Silu).then_inc(silu_done, 1)
                        weight_hi(u0 + 3 + 2 * f, 1)
                        act.wait_ge(prod_done, f + (f0 + 1))
                        A(CH[:, bass.ds(f, 1), :].rearrange("p a t -> p (a t)"), T[3],
                          ACT.Copy).then_inc(a_hi, 1)
                    d0 = U_DOWN[l][c]
                    for m in range(KT):
                        u = d0 + m
                        if c == 0:
                            act.wait_ge(mm_done, u + 1)
                            A(Y[:, m, :], PS[u % 2][:, :], ACT.Copy).then_inc(y_first, 1)
                        if c == 2:
                            act.wait_ge(y_part, 16 * l + 8 + m + 1)
                            square(4 * l + 3, m, Y[:, m, :])
                        ahead(u)
                root(N_Y[2 * l + 1], S, RSTD)

            sub_layer(0)
            residual(2)
            root(N_X[2], S, RSTD)

            memory(1)
            memory_kv(1)
            act.wait_ge(ang_ready, 1)
            A(SIN[:, :], T[0], ACT.Sin).then_inc(trig_done, 1)
            act.wait_ge(ang_ready, 2)
            A(COS[:, :], T[1], ACT.Sin, scale=-1.0, bias=CN[:, C_HPI:C_HPI + 1]).then_inc(trig_done, 1)
            for m in range(2 * NMT):
                u = U_KV + m
                if m < NMT:
                    act.wait_ge(cos_part, m + 1)
                    halves_swapped(u)
                ahead(u)
                if m < NMT:
                    act.wait_ge(roped, m + 1)
                    src = T[2]
                else:
                    act.wait_ge(v_tr, m - NMT + 1)
                    src = PV2[:, :]
                if m:
                    act.wait_ge(spilled, 32 * m)
                A(STG[0][:, :], src, ACT.Copy).then_inc(st_hi, 1)
            for m in range(KT):
                u = U_IN[1] + m
                if m < NMT:
                    act.wait_ge(cos_part, NMT + m + 1)
                    halves_swapped(u)
                ahead(u)
                if m < NMT:
                    tile_hi(n_tile - 8, CH[:, m, :], T[2])
                else:
                    tile_hi(n_tile - 8, CH[:, m, :], T[3])
                n_tile += 1
            attention([2, 3], 32, lambda *a: None)
            for m in range(2):
                act.wait_ge(o_free, 8 + 4 * (m + 1))
                A(CH[:, NMT + m, :], T[1] if m else T[0], ACT.Copy).then_inc(c_hi, 1)

            def spread(a, sl, h, n):
                o = a // 4
                g = SLOTS[sl][2] // 2
                d, half = DIL[g], n // 4
                rr = slice(half * d // 2, (half + 1) * d // 2) if d > 1 else slice(0, 1)
                act.wait_ge(pv_done, a + 1)
                if o == 16:
                    act.wait_ge(c_lo, 26)
                for dst, row in ((OB[g][:, :], h), (LB[g][:, :], 1 - h)):
                    cols = dst[DH * h:DH * (h + 1), :]
                    if d > 1:
                        cols = sorted_cols(cols, g)[:, rr, :]
                        bank = PO[o % 2][DH * row:DH * (row + 1), :].rearrange("p (r l) -> p r l", r=d // 2)
                    else:
                        cols = cols[:, HB * half:HB * (half + 1)]
                        bank = PO[o % 2][DH * row:DH * (row + 1), :]
                    A(cols, bank, ACT.Copy).then_inc(o_free, 1)

            for pair in range(2):
                for g in range(3):
                    i = 3 * pair + g
                    attention([4 + i], 64 + 16 * i, spread)
                    act.wait_ge(mb_tr, i + 1)
                    src = PN[:, :]
                    if DIL[g] > 1:
                        A(sorted_cols(MB[g], g), src.rearrange("p (r l) -> p r l", r=DIL[g]),
                          ACT.Copy).then_inc(mb_out, 1)
                    else:
                        A(MB[g], src, ACT.Copy).then_inc(mb_out, 1)
                for g in range(3):
                    act.wait_ge(mdiff, 3 * pair + g + 1)
                    A(MB[g], MB[g], ACT.Exp, scale=SCALE).then_inc(mexp, 1)
                for g in range(3):
                    act.wait_ge(mix_ready, 16 + 3 * pair + g + 1)
                    A(CH[:, 2 * g + pair, :], OB[g][:, :], ACT.Copy).then_inc(c_hi, 1)
            for u in (U_OUT1, U_OUT1 + 1):
                weight_hi(u, u % 2)
            sub_layer_done = sub_layer(1)

        @block.tensor
        def _(pe):
            MM = nc.tensor.matmul

            def unit(u, slot, ks, rh, rl, width=S, wait_k=None, free=None):
                pe.wait_ge(w_lo, u + 1)
                if free is None and u >= 2:
                    free = released(u - 2)
                if free is not None:
                    pe.wait_ge(*free)
                halves = [(0, HB), (HB, S)] if width == S else [(0, width)]
                for i, k in enumerate(ks):
                    if wait_k is not None:
                        wait_k(k)
                    last = i == len(ks) - 1
                    for a, b in halves:
                        MM(PS[slot][:, a:b], WH[:, slot, k, :], rh(k)[:, a:b], start=(i == 0), stop=False)
                        MM(PS[slot][:, a:b], WH[:, slot, k, :], rl(k)[:, a:b], start=False, stop=False)
                    for a, b in halves:
                        ins = MM(PS[slot][:, a:b], WL[:, slot, k, :], rh(k)[:, a:b], start=False, stop=last)
                ins.then_inc(mm_done, 1)

            def stream(part):
                return lambda k: part[:, k, :]

            def norm(width, source, count, n, free=None):
                pe.wait_ge(source, count)
                if n >= 1:
                    pe.wait_ge(norm_root, n)
                for a in range(0, width, HB):
                    b = min(a + HB, width)
                    ins = MM(PN[:, a:b], ONES, SS[:, a:b], start=True, stop=True)
                ins.then_inc(norm_sum, 1)

            def memory(l):
                norm(MEM, mem_ss, l + 1, N_MEM[l])
                pe.wait_ge(mem_lo, l + 1)
                mt = [c[:, 0:2, :].rearrange("p a (b t) -> p (a b) t", b=4) for c in (CH, CL)]
                for m in range(4):
                    u = U_MEM[l] + m
                    unit(u, u % 2, range(KT), stream(mt[0]), stream(mt[1]), width=MEM)

            def memory_values(l):
                for m in range(2):
                    pe.wait_ge(mem_scaled, 4 * l + 2 + m + 1)
                    for i in range(2):
                        c = (2 + m) * MEM + i * P
                        ins = nc.tensor.transpose(PV2[:, (2 * i + m) * P:(2 * i + m + 1) * P],
                                                  TP[2][:, c:c + P], IDENT)
                    ins.then_inc(vm_tr, 1)

            def attention(slots, a0, free_o):
                tiles = [(sl, h, n) for sl in slots for h in range(2) for n in range(8)]
                for i in range(len(tiles) + 2):
                    if i < len(tiles):
                        a = a0 + i
                        sl, h, n = tiles[i]
                        t = SLOTS[sl][2]
                        k0, nk, _ = key_span(sl, n)
                        rows = slice(DH * h, DH * (h + 1))
                        kk = [KM[j][rows, t - NMT, :] for j in range(2)] if SLOTS[sl][0] == "mem" \
                            else [KA[j][rows, k0:k0 + nk] for j in range(2)]
                        qq = [c[rows, t, P * n:P * (n + 1)] for c in (CH, CL)]
                        lag(pe, exp_done, a + 1, 2)
                        for j, (x, y) in enumerate(((0, 0), (0, 1), (1, 0))):
                            ins = MM(PSC[a % 2][:, 0:nk], qq[x], kk[y], start=(j == 0), stop=(j == 2))
                        ins.then_inc(scored, 1)
                    if 1 <= i <= len(tiles):
                        a = a0 + i - 1
                        nk = key_span(tiles[i - 1][0], tiles[i - 1][2])[1]
                        pe.wait_ge(exp_done, a + 1)
                        lag(pe, pt_lo, a + 1, 2)
                        for j in range(nk // P):
                            ins = nc.tensor.transpose(PTR[a % 2][:, P * j:P * (j + 1)],
                                                      PR[:, a % 2, P * j:P * (j + 1)], IDENT)
                        ins.then_inc(p_tr, 1)
                    if i >= 2:
                        a = a0 + i - 2
                        sl, h, n = tiles[i - 2]
                        t = SLOTS[sl][2]
                        k0, nk, _ = key_span(sl, n)
                        o = a // 4
                        pe.wait_ge(pt_lo, a + 1)
                        if a % 4 == 0 and o >= 2:
                            pe.wait_ge(o_free, outputs_out(o - 2))
                        vc = slice(DH * h, DH * h + P)
                        steps = []
                        for j in range(nk // P):
                            vv = [VM[x][:, j, t - NMT, vc] for x in range(2)] if SLOTS[sl][0] == "mem" \
                                else [VA[x][:, k0 // P + j, vc] for x in range(2)]
                            pp = [PT[x][:, a % 2, P * j:P * (j + 1)] for x in range(2)]
                            steps += [(vv[0], pp[0]), (vv[0], pp[1]), (vv[1], pp[0])]
                        for j, (v, p) in enumerate(steps):
                            ins = MM(PO[o % 2][:, P * (a % 4):P * (a % 4 + 1)], v, p,
                                     start=(j == 0), stop=(j == len(steps) - 1))
                        ins.then_inc(pv_done, 1)

            pe.wait_ge(consts_in, 32)
            memory(0)
            memory_values(0)
            norm(S, ss_done, 8, N_X[0])
            for m in range(KT):
                u = U_IN[0] + m
                if m == 0:
                    pe.wait_ge(x_lo, 8)
                unit(u, u % 2, range(KT), stream(XH), stream(XL))
            for m in range(NMT):
                u = U_POOL + m
                t, j = m // 3, m % 3
                ks = ((0, 1), (0, 1, 2), (1, 2))[j]
                pe.wait_ge(c_lo, 3 * t + 3)
                unit(u, u % 2, ks, lambda k, t=t: CH[:, 3 * t + k, :], lambda k, t=t: CL[:, 3 * t + k, :])
            for u in (U_POOL + NMT - 2, U_POOL + NMT - 1):
                pe.wait_ge(*released(u))
            pe.wait_ge(c_lo, 8)
            pe.wait_ge(vm_lo, 2)
            pe.wait_ge(km_lo, 2)
            attention([0, 1], 0, None)

            def ffn(l):
                for c, nf in enumerate(CHUNKS):
                    u0, f0 = U_FFN[l][c], 22 * l + 8 * c
                    for j in range(2):
                        unit(u0 + j, j, range(KT), stream(XH), stream(XL))
                    with pe.Fori(1, nf) as f:
                        for j, s in enumerate((silu_in, up_scaled)):
                            unit(2 * f + (u0 + j), j, range(KT), stream(XH), stream(XL), free=(s, f + f0))
                    d0 = U_DOWN[l][c]
                    for m in range(KT):
                        u = d0 + m
                        if m == 0:
                            unit(u, u % 2, range(nf), stream(CH), stream(CL),
                                 wait_k=lambda k: pe.wait_ge(a_lo, f0 + k + 1))
                        else:
                            unit(u, u % 2, range(nf), stream(CH), stream(CL))

            def sub_layer(l):
                for m in range(KT):
                    u = U_OUT[l] + m
                    if m == 0:
                        pe.wait_ge(c_lo, 16 if l == 0 else 32)
                        pe.wait_ge(pt_lo, 32 if l == 0 else 160)
                    unit(u, u % 2, range(KT), stream(CH), stream(CL))
                norm(S, ss_done, 8 * (SERIES_OF[N_Y[2 * l]] + 1), N_Y[2 * l])
                pe.wait_ge(x_lo, 8 * (2 * l + 2))
                norm(S, ss_done, 8 * (SERIES_OF[N_X[2 * l + 1]] + 1), N_X[2 * l + 1])
                ffn(l)
                norm(S, ss_done, 8 * (SERIES_OF[N_Y[2 * l + 1]] + 1), N_Y[2 * l + 1])

            sub_layer(0)
            pe.wait_ge(x_lo, 24)
            norm(S, ss_done, 8 * 5, N_X[2])
            memory(1)
            memory_values(1)
            for m in range(2 * NMT):
                u = U_KV + m
                unit(u, u % 2, range(KT), stream(XH), stream(XL))
                if m >= NMT:
                    i = m - NMT
                    pe.wait_ge(v_scaled, i + 1)
                    if i == 0:
                        pe.wait_ge(vm_lo, 4)
                    else:
                        pe.wait_ge(st_lo, m)
                    for n in range(8):
                        ins = nc.tensor.transpose(PV2[:, P * n:P * (n + 1)], T[3][:, P * n:P * (n + 1)], IDENT)
                    ins.then_inc(v_tr, 1)
            for m in range(KT):
                u = U_IN[1] + m
                unit(u, u % 2, range(KT), stream(XH), stream(XL))
            for u in (U_OUT1 - 2, U_OUT1 - 1):
                pe.wait_ge(*released(u))
            pe.wait_ge(c_lo, 24)
            pe.wait_ge(km_lo, 4)
            pe.wait_ge(st_lo, 12)
            attention([2, 3], 32, None)
            for i in range(6):
                pe.wait_ge(kv_in, 16 * 6 * (i + 1))
                attention([4 + i], 64 + 16 * i, None)
                pe.wait_ge(mb_cast, i + 1)
                if i:
                    pe.wait_ge(mb_out, i)
                mx = TP[3][:, PAD:PAD + S]
                for n in range(8):
                    ins = nc.tensor.transpose(PN[:, P * n:P * (n + 1)], mx[:, P * n:P * (n + 1)], IDENT)
                ins.then_inc(mb_tr, 1)
            sub_layer(1)

        @block.vector
        def _(dve):
            V = nc.vector
            own = [0]

            def link(ins):
                own[0] += 1
                ins.then_inc(dve_own, 1)
                dve.wait_ge(dve_own, own[0])

            def weight_lo(u, slot, k=KT):
                dve.wait_ge(w_hi, u + 1)
                V.tensor_tensor(WL[:, slot, 0:k, :], WR[:, slot, 0:k, :], as_f32(WH[:, slot, 0:k, :]),
                                ALU.subtract).then_inc(w_lo, 1)

            def ahead(u):
                v = u + 2
                if v < NU and v not in (U_OUT1, U_OUT1 + 1):
                    weight_lo(v, v % 2, UNITS[v][3])

            def norm_finish(n, width, dst):
                dve.wait_ge(norm_root, n + 1)
                V.reciprocal(dst[:, 0:width], dst[:, 0:width]).then_inc(norm_done, 1)

            def residual(j):
                for k in range(KT + 1):
                    if k < KT and j > 0:
                        dve.wait_ge(norm_done, N_Y[j - 1] + 1)
                        if j in (1, 3):
                            dve.wait_ge(y_first, 16 * (j // 2) + k + 1)
                        else:
                            dve.wait_ge(sq_done, 8 * (4 * (j // 2 - 1) + 3) + k + 1)
                        link(V.tensor_tensor(Y[:, k, :], Y[:, k, :], RSTD[:, :], ALU.mult))
                        dve.wait_ge(x_sum, 8 * (j - 1) + k + 1)
                        gcol = 8 * (4 * ((j - 1) // 2) + (1 if j % 2 else 3)) + k
                        V.scalar_tensor_tensor(out=Y[:, k, :], in0=Y[:, k, :], scalar=GN[:, gcol:gcol + 1],
                                               in1=T[k % 2], op0=ALU.mult, op1=ALU.add).then_inc(res_done, 1)
                    if k >= 1 and j < 4:
                        q = k - 1
                        dve.wait_ge(x_hi, 8 * j + q + 1)
                        V.tensor_tensor(XL[:, q, :], Y[:, q, :], as_f32(XH[:, q, :]),
                                        ALU.subtract).then_inc(x_lo, 1)

            def memory(l):
                dve.wait_ge(mem_sq, l + 1)
                if l:
                    dve.wait_ge(norm_sum, N_X[2] + 1)
                V.tensor_reduce(SS[:, 0:MEM], MS[:, :, :].rearrange("p k t -> p t k"), AX_X,
                                ALU.add).then_inc(mem_ss, 1)
                dve.wait_ge(mem_hi, l + 1)
                V.tensor_tensor(CL[:, 0:2, :].rearrange("p a (b t) -> p (a b) t", b=4), MR[:, :, :],
                                as_f32(CH[:, 0:2, :].rearrange("p a (b t) -> p (a b) t", b=4)),
                                ALU.subtract).then_inc(mem_lo, 1)

            def memory_kv(l):
                norm_finish(N_MEM[l], MEM, RSTDM)
                dve.wait_ge(norm_done, N_MEM[l] + 1)
                if l == 0:
                    dve.wait_ge(ss_done, 8)
                for m in range(4):
                    u = U_MEM[l] + m
                    dve.wait_ge(mm_done, u + 1)
                    V.tensor_tensor(TP[2][:, m * MEM:(m + 1) * MEM], PS[u % 2][:, 0:MEM], RSTDM[:, :],
                                    ALU.mult).then_inc(mem_scaled, 1)
                    dve.wait_ge(mem_scaled, 4 * l + m + 1)
                    if m < 2:
                        dve.wait_ge(km_hi, 2 * l + m + 1)
                        V.tensor_tensor(KM[1][:, m, :], TP[2][:, m * MEM:(m + 1) * MEM],
                                        as_f32(KM[0][:, m, :]),
                                        ALU.subtract).then_inc(km_lo, 1)
                    ahead(u)
                for i in range(2):
                    dve.wait_ge(vm_hi, 2 * l + 2)
                    out = VM[1][:, i, :, :].rearrange("p a (h c) -> p a h c", h=3)[:, :, 0:3:2, :]
                    hi = VM[0][:, i, :, :].rearrange("p a (h c) -> p a h c", h=3)[:, :, 0:3:2, :]
                    V.tensor_tensor(out, PV2[:, 2 * P * i:2 * P * (i + 1)].rearrange(
                        "p (a h c) -> p a h c", a=2, h=2), as_f32(hi), ALU.subtract).then_inc(vm_lo, 1)

            def tile_lo(n, m, src):
                dve.wait_ge(c_hi, n + 1)
                V.tensor_tensor(CL[:, m, :], src, as_f32(CH[:, m, :]), ALU.subtract).then_inc(c_lo, 1)
                dve.wait_ge(c_lo, n + 1)

            def attention(slots, a0):
                tiles = [(sl, h, n) for sl in slots for h in range(2) for n in range(8)]
                mem = SLOTS[slots[0]][0] == "mem"
                for i in range(len(tiles) + 2):
                    if i < len(tiles):
                        a = a0 + i
                        sl, h, n = tiles[i]
                        _, nk, mask = key_span(sl, n)
                        dve.wait_ge(scored, a + 1)
                        lag(dve, exp_done, a + 1, 2)
                        mcol = MC[:, h, n:n + 1]
                        if mem:
                            link(V.tensor_reduce(mcol, PSC[a % 2][:, 0:nk], AX_X, ALU.max))
                        else:
                            link(V.tensor_tensor_reduce(SM[:, a % 2, 0:nk], PSC[a % 2][:, 0:nk],
                                                        MK[:, mask[0]:mask[1]], 1.0, NEG, ALU.add,
                                                        ALU.max, mcol))
                        V.tensor_scalar(NM[:, a % 2:a % 2 + 1], mcol, -SCALE, None,
                                        ALU.mult).then_inc(max_done, 1)
                    if 1 <= i <= len(tiles):
                        a = a0 + i - 1
                        nk = key_span(tiles[i - 1][0], tiles[i - 1][2])[1]
                        dve.wait_ge(pt_hi, a + 1)
                        V.tensor_tensor(PT[1][:, a % 2, 0:nk], PTR[a % 2][:, 0:nk], as_f32(PT[0][:, a % 2, 0:nk]),
                                        ALU.subtract).then_inc(pt_lo, 1)
                    if mem and i >= 2 and (i - 2) % 4 == 3:
                        a = a0 + i - 2
                        sl, h, n = tiles[i - 2]
                        m = SLOTS[sl][2] - NMT
                        o, half = a // 4, n // 4
                        dve.wait_ge(pv_done, a + 1)
                        rows, others = slice(DH * h, DH * h + DH), slice(DH * (1 - h), DH * (1 - h) + DH)
                        link(V.reciprocal(T[2][rows, 0:HB], PO[o % 2][others, :]))
                        dst = T[m]
                        V.tensor_tensor(dst[rows, HB * half:HB * (half + 1)], PO[o % 2][rows, :],
                                        T[2][rows, 0:HB], ALU.mult).then_inc(o_free, 1)

            dve.wait_ge(consts_in, 32)
            memory(0)
            for u in range(2):
                weight_lo(u, u)
            residual(0)
            memory_kv(0)
            norm_finish(N_X[0], S, RSTD)
            dve.wait_ge(norm_done, N_X[0] + 1)
            dve.wait_ge(pads_zero, 3)

            n_tile = 0
            for m in range(KT):
                u = U_IN[0] + m
                dve.wait_ge(mm_done, u + 1)
                if m < NMT:
                    V.tensor_tensor(T[0], PS[u % 2][:, :], RSTD[:, :], ALU.mult).then_inc(in_scaled, 1)
                    dve.wait_ge(in_scaled, m + 1)
                    ahead(u)
                    dve.wait_ge(pooled, m + 1)
                    nlev = len({WINDOWS[(m * P + r) // POOLG] for r in range(P)} and
                               [w for w in WINDOWS if w <= WINDOWS[(m * P + P - 1) // POOLG]])
                    src = T[1 + (nlev - 1) % 2]
                    V.scalar_tensor_tensor(out=T[3], in0=src, scalar=CN[:, C_INVW + m:C_INVW + m + 1],
                                           in1=T[0], op0=ALU.mult,
                                           op1=ALU.subtract).then_inc(mix_ready, 1)
                else:
                    V.tensor_tensor(T[3], PS[u % 2][:, :], RSTD[:, :], ALU.mult).then_inc(mix_ready, 1)
                    dve.wait_ge(mix_ready, m + 1)
                    ahead(u)
                dve.wait_ge(mix_ready, m + 1)
                tile_lo(n_tile, m, T[3])
                n_tile += 1
            for m in range(NMT):
                ahead(U_POOL + m)
            for m in range(NMT):
                tile_lo(n_tile, m, Y[:, m, :])
                n_tile += 1
            attention([0, 1], 0)
            for m in range(2):
                tile_lo(n_tile, NMT + m, T[m])
                n_tile += 1

            def sub_layer(l):
                for m in range(KT):
                    ahead(U_OUT[l] + m)
                norm_finish(N_Y[2 * l], S, RSTD)
                residual(2 * l + 1)
                norm_finish(N_X[2 * l + 1], S, RSTD)
                dve.wait_ge(norm_done, N_X[2 * l + 1] + 1)
                dve.wait_ge(ss_done, 8 * (SERIES_OF[N_X[2 * l + 1]] + 1))
                for c, nf in enumerate(CHUNKS):
                    u0, f0 = U_FFN[l][c], 22 * l + 8 * c
                    with dve.Fori(0, nf) as f:
                        dve.wait_ge(mm_done, 2 * f + (u0 + 1))
                        V.tensor_tensor(T[0], PS[0][:, :], RSTD[:, :], ALU.mult).then_inc(silu_in, 1)
                        dve.wait_ge(silu_in, f + (f0 + 1))
                        weight_lo(u0 + 2 + 2 * f, 0)
                        dve.wait_ge(mm_done, 2 * f + (u0 + 2))
                        V.tensor_tensor(T[2], PS[1][:, :], RSTD[:, :], ALU.mult).then_inc(up_scaled, 1)
                        dve.wait_ge(up_scaled, f + (f0 + 1))
                        dve.wait_ge(silu_done, f + (f0 + 1))
                        V.tensor_tensor(T[3], T[1], T[2], ALU.mult).then_inc(prod_done, 1)
                        weight_lo(u0 + 3 + 2 * f, 1)
                        dve.wait_ge(a_hi, f + (f0 + 1))
                        V.tensor_tensor(CL[:, bass.ds(f, 1), :].rearrange("p a t -> p (a t)"), T[3],
                                        as_f32(CH[:, bass.ds(f, 1), :].rearrange("p a t -> p (a t)")),
                                        ALU.subtract).then_inc(a_lo, 1)
                        dve.wait_ge(a_lo, f + (f0 + 1))
                    for m in range(KT):
                        u = U_DOWN[l][c] + m
                        if c:
                            dve.wait_ge(mm_done, u + 1)
                            if c == 1:
                                dve.wait_ge(y_first, 16 * l + 8 + m + 1)
                            else:
                                dve.wait_ge(y_part, 16 * l + m + 1)
                            V.tensor_tensor(Y[:, m, :], Y[:, m, :], PS[u % 2][:, :],
                                            ALU.add).then_inc(y_part, 1)
                            dve.wait_ge(y_part, 16 * l + 8 * (c - 1) + m + 1)
                        ahead(u)
                norm_finish(N_Y[2 * l + 1], S, RSTD)
                residual(2 * l + 2)

            sub_layer(0)
            norm_finish(N_X[2], S, RSTD)
            dve.wait_ge(norm_done, N_X[2] + 1)

            memory(1)
            memory_kv(1)
            two_pi = 2.0 * np.pi
            c1 = 6.28125
            c2 = float(np.float32(np.round((two_pi - c1) * 2 ** 21) / 2 ** 21))
            c3 = float(np.float32(two_pi - c1 - c2))
            pi_below = 3.1415925
            dve.wait_ge(pos_in, 16)
            link(V.tensor_copy(T[0], POS[:, :]))
            link(V.tensor_scalar(T[0], T[0], CN[:, C_FREQ:C_FREQ + 1], None, ALU.mult))
            link(V.tensor_scalar(T[1], T[0], float(1.0 / two_pi), SUMROW, ALU.mult, ALU.add))
            link(V.tensor_scalar(T[1], T[1], SUMROW, None, ALU.subtract))
            for part in (c1, c2, c3):
                link(V.scalar_tensor_tensor(out=T[0], in0=T[1], scalar=-part, in1=T[0],
                                            op0=ALU.mult, op1=ALU.add))
            link(V.tensor_scalar(T[0], T[0], pi_below, -pi_below, ALU.min, ALU.max))
            V.tensor_scalar(T[1], T[0], -1.0, None, ALU.mult).then_inc(ang_ready, 1)
            dve.wait_ge(ang_ready, 1)
            V.tensor_tensor(T[1], T[1], T[0], ALU.max).then_inc(ang_ready, 1)
            dve.wait_ge(trig_done, 2)
            link(V.scalar_tensor_tensor(out=SIN[:, :], in0=SIN[:, :], scalar=CN[:, C_SIGN:C_SIGN + 1],
                                        in1=RSTD[:, :], op0=ALU.mult, op1=ALU.mult))
            link(V.tensor_tensor(COS[:, :], COS[:, :], RSTD[:, :], ALU.mult))

            def rotate(u, n, g, done):
                V.tensor_tensor(T[0], PS[u % 2][:, :], COS[:, :], ALU.mult).then_inc(cos_part, 1)
                ahead(u)
                dve.wait_ge(swapped, n + 1)
                link(V.tensor_tensor(T[1], T[1], SIN[:, :], ALU.mult))
                dve.wait_ge(cos_part, n + 1)
                if DIL[g] > 1:
                    V.tensor_tensor(T[2].rearrange("p (r l) -> p r l", r=DIL[g]), sorted_cols(T[0], g),
                                    sorted_cols(T[1], g), ALU.add).then_inc(done, 1)
                else:
                    V.tensor_tensor(T[2], T[0], T[1], ALU.add).then_inc(done, 1)

            for m in range(2 * NMT):
                u = U_KV + m
                dve.wait_ge(mm_done, u + 1)
                if m < NMT:
                    rotate(u, m, m // 2, roped)
                    dve.wait_ge(roped, m + 1)
                    src = T[2]
                else:
                    if m > NMT:
                        dve.wait_ge(v_tr, m - NMT)
                    g = (m - NMT) // 2
                    if DIL[g] > 1:
                        V.tensor_tensor(T[3].rearrange("p (r l) -> p r l", r=DIL[g]),
                                        sorted_cols(PS[u % 2][:, :], g), sorted_cols(RSTD[:, :], g),
                                        ALU.mult).then_inc(v_scaled, 1)
                    else:
                        V.tensor_tensor(T[3], PS[u % 2][:, :], RSTD[:, :], ALU.mult).then_inc(v_scaled, 1)
                    dve.wait_ge(v_scaled, m - NMT + 1)
                    ahead(u)
                    src = PV2[:, :]
                dve.wait_ge(st_hi, m + 1)
                V.tensor_tensor(STG[1][:, :], src, as_f32(STG[0][:, :]), ALU.subtract).then_inc(st_lo, 1)
            for m in range(KT):
                u = U_IN[1] + m
                dve.wait_ge(mm_done, u + 1)
                if m < NMT:
                    rotate(u, NMT + m, m // 2, mix_ready)
                    dve.wait_ge(mix_ready, 8 + m + 1)
                    tile_lo(16 + m, m, T[2])
                else:
                    V.tensor_tensor(T[3], PS[u % 2][:, :], RSTD[:, :], ALU.mult).then_inc(mix_ready, 1)
                    dve.wait_ge(mix_ready, 8 + m + 1)
                    ahead(u)
                    tile_lo(16 + m, m, T[3])
            attention([2, 3], 32)
            for m in range(2):
                tile_lo(24 + m, NMT + m, T[m])
            dve.wait_ge(mask_in, 16)
            for pair in range(2):
                for g in range(3):
                    i = 3 * pair + g
                    attention([4 + i], 64 + 16 * i)
                    if i:
                        dve.wait_ge(mb_tr, i)
                    V.tensor_copy(T[3].rearrange("p (n h c) -> p n h c", n=8, h=2),
                                  MC[:, :, :].rearrange("p h n -> p n h").unsqueeze(3)
                                  .to_broadcast([P, 8, 2, DH])).then_inc(mb_cast, 1)
                dve.wait_ge(mb_out, 3 * pair + 3)
                dve.wait_ge(o_free, outputs_out(16 + 12 * (pair + 1) - 1))
                link(V.tensor_tensor(T[3], MB[0], MB[1], ALU.max))
                link(V.tensor_tensor(T[3], T[3], MB[2], ALU.max))
                for g in range(3):
                    V.tensor_tensor(MB[g], MB[g], T[3], ALU.subtract).then_inc(mdiff, 1)
                for g in range(3):
                    dve.wait_ge(mexp, 3 * pair + g + 1)
                    link(V.tensor_tensor(LB[g][:, :], LB[g][:, :], MB[g], ALU.mult))
                link(V.tensor_tensor(LB[0][:, :], LB[0][:, :], LB[1][:, :], ALU.add))
                link(V.tensor_tensor(LB[0][:, :], LB[0][:, :], LB[2][:, :], ALU.add))
                link(V.reciprocal(LB[0][:, :], LB[0][:, :]))
                for g in range(3):
                    link(V.tensor_tensor(MB[g], MB[g], LB[0][:, :], ALU.mult))
                    V.tensor_tensor(OB[g][:, :], OB[g][:, :], MB[g], ALU.mult).then_inc(mix_ready, 1)
                    dve.wait_ge(mix_ready, 16 + 3 * pair + g + 1)
                for g in range(3):
                    tile_lo(26 + 3 * pair + g, 2 * g + pair, OB[g][:, :])
            for u in (U_OUT1, U_OUT1 + 1):
                weight_lo(u, u % 2)
            sub_layer(1)


def pack_units(inp):
    w_all = np.zeros((NU, P, KT * P), np.float32)
    pool = np.zeros((2, 3 * P, 3 * P), np.float32)
    for g in range(4):
        r = (g % 2) * POOLG
        pool[g // 2, r:r + POOLG, r:r + POOLG] = inp["w_pool"][0, g]
    f0s = (0, 8, 16)
    for u, (name, l, i, k, _) in enumerate(UNITS):
        if name == "mem":
            w = inp["w_mem_kv"][l][:, P * i:P * (i + 1)]
        elif name == "kv":
            w = inp["w_kv"][:, P * i:P * (i + 1)]
        elif name == "in":
            w = inp["w_in"][l][:, P * i:P * (i + 1)]
        elif name == "pool":
            w = pool[i // 3][:, P * (i % 3):P * (i % 3 + 1)]
        elif name == "out":
            w = inp["w_out"][l][:, P * i:P * (i + 1)]
        elif name == "ffn":
            _, f, j = i
            w = inp["w_gate_up"][l][:, j * DFF + P * f:j * DFF + P * (f + 1)]
        else:
            c, m = i
            w = inp["w_down"][l][P * f0s[c]:P * (f0s[c] + k), P * m:P * (m + 1)]
        w_all[u, :, 0:k * P] = w.reshape(k, P, P).transpose(1, 0, 2).reshape(P, k * P)
    return w_all


def constant_tables():
    c = np.zeros((P, NCONST), np.float32)
    c[:, C_ID:C_ID + P] = np.eye(P)
    c[:, C_ONE:C_ONE + P] = 1.0
    p = np.arange(P)
    for m in range(NMT):
        w = np.array(WINDOWS)[(m * P + p) // POOLG]
        c[:, C_INVW + m] = 1.0 / w
        for t in range(PAD):
            c[:, C_EDGE + PAD * m + t] = w / np.minimum(t + 1, w)
    half = DH // 2
    freqs = np.float32(10000.0) ** (-np.arange(half, dtype=np.float32) / half)
    c[:, C_FREQ] = freqs[p % half]
    c[:, C_SIGN] = np.where(p % DH < half, -1.0, 1.0)
    c[:, C_EPS] = EPS
    c[:, C_HPI] = np.pi / 2
    q, k = np.meshgrid(p, p, indexing="ij")
    prev = np.where(k >= q, 0.0, NEG)
    causal = np.where(k <= q, 0.0, NEG)
    by_residue = np.where((k <= q) & (k // 64 == q // 64), 0.0, NEG)
    return c, np.concatenate([prev, causal, by_residue], 1).astype(np.float32)


def kernel(**inputs):
    import concourse.bacc as bacc
    from concourse.bass_utils import run_bass_kernel_spmd

    inp = {k: np.asarray(v) for k, v in inputs.items()}
    tiles = lambda a: np.ascontiguousarray(a.T.reshape(KT, P, -1).transpose(1, 0, 2))
    columns = lambda a: a.reshape(-1, P).T
    consts, masks = constant_tables()
    gains = np.concatenate([columns(inp["norm_gains"]), columns(inp["mem_norm"]), columns(inp["kv_norm"]),
                            columns(inp["pool_scale"])], 1)
    arrays = {
        "in_w": pack_units(inp),
        "in_x": tiles(inp["x"][0]),
        "in_mem": tiles(inp["mem"][0]),
        "in_pos": np.ascontiguousarray(inp["positions"]),
        "in_gains": np.ascontiguousarray(gains),
        "in_consts": consts,
        "in_masks": masks,
    }
    nc = bacc.Bacc("TRN2", target_bir_lowering=False, num_devices=1, dynamic_dma_scratch_size=1024)
    aps = [nc.dram_tensor(n, a.shape, mybir.dt.from_np(a.dtype), kind="ExternalInput").ap()
           for n, a in arrays.items()]
    k_scr = nc.dram_tensor("k_scratch", (NMT, 2, P, S), F32, kind="Internal").ap()
    v_scr = nc.dram_tensor("v_scratch", (NMT, 2, P, S), F32, kind="Internal").ap()
    out_t = nc.dram_tensor("out_t", (P, KT, S), F32, kind="ExternalOutput").ap()
    build(nc, *aps, k_scr, v_scr, out_t)
    got = run_bass_kernel_spmd(nc, [arrays], core_ids=[0]).results[0]["out_t"]
    return np.ascontiguousarray(got.transpose(1, 0, 2).reshape(D, S).T)[None]
```

```python
from contextlib import ExitStack

import numpy as np

import concourse.bass as bass
from concourse import mybir

F32 = mybir.dt.float32
F32R = mybir.dt.float32r
I32 = mybir.dt.int32
ALU = mybir.AluOpType
ACT = mybir.ActivationFunctionType
AX_X = mybir.AxisListType.X

P = 128
D = 1024
S = 1024
KT = D // P
HT = S // 2
MEM = 256
DH = 64
MAIN = 768
NMT = MAIN // P
DFF = 2816
CHUNKS = (8, 8, 6)
CH0 = (0, 8, 16)
WINDOWS = (2, 4, 8, 16)
POOLG = MAIN // 4
DIL = (1, 4, 16)
PAD = 16
EPS = 1e-6
SCALE = DH ** -0.5
NEG = -1e30
ROUND = 1.5 * 2.0 ** 23
OUT_ORDER = ((3, 4, 5, 0, 1, 2, 6, 7), (6, 7, 0, 2, 4, 1, 3, 5))
POOL_IN = (3, 4, 5, 1, 2, 0)
POOL_OUT = (3, 4, 5, 0, 1, 2)
NHT = 4
RES_AT = ((0,), (1, 2), (3,), (4, 5), (6,), (7,), (), ())
RES_FFN = ((0,), (1,), (2,), (3,), (4,), (5,), (6,), (7,))
HALF = (slice(0, HT), slice(HT, S))

G_POOL = 8 * 11
NGAIN = G_POOL + NMT
C_ID = 0
C_ONE = C_ID + P
C_EDGE = C_ONE + 8
C_INVW = C_EDGE + NMT * PAD
C_FREQ = C_INVW + NMT
C_SIGN = C_FREQ + 1
C_EPS = C_SIGN + 1
C_HPI = C_EPS + 1
NCONST = C_HPI + 1


def as_f32(ap):
    return ap.bitcast(F32)


def weight_rows():
    rows = []
    for l in range(2):
        rows += [("mem", l, m) for m in range(4)]
        rows += [("in", l, m) for m in (6, 7) + (POOL_IN if l == 0 else tuple(range(NMT)))]
        rows += [("pool", 0, m) for m in POOL_OUT] if l == 0 else [("kv", 1, m) for m in range(2 * NMT)]
        rows += [("out", l, m) for m in range(KT)]
        for c, n in enumerate(CHUNKS):
            rows += [("ffn", l, (f, j)) for f in range(CH0[c], CH0[c] + n) for j in range(2)]
            rows += [("down", l, (c, m)) for m in range(KT)]
    return rows


ROWS = weight_rows()
ROW = {r: i for i, r in enumerate(ROWS)}


class Job:

    def __init__(self, name, l, i, k0=0, kn=KT, gain=None, halves=(0, 1), tag=None):
        self.name, self.l, self.i, self.k0, self.kn = name, l, i, k0, kn
        self.gain, self.halves, self.tag = gain, halves, tag
        self.row = ROW[(name, l, i)]
        self.key = (name, l, i, tag)


def plan_jobs():
    jobs = []
    for l in range(2):
        jobs += [Job("mem", l, m, gain=8 + l) for m in range(4)] if l == 0 else []
        if l == 0:
            jobs += [Job("in", 0, m, gain=0) for m in (6, 7) + POOL_IN]
            jobs += [Job("pool", 0, m, kn=3) for m in POOL_OUT]
            jobs += [Job("out", 0, m, halves=(h,), tag=h) for h in range(2) for m in range(KT)]
        else:
            jobs += [Job("in", 1, m, gain=4, halves=(0,), tag=0) for m in (6, 7)]
            jobs += [Job("mem", 1, m, gain=9) for m in range(4)]
            jobs += [Job("in", 1, m, gain=4, halves=(1,), tag=1) for m in (6, 7)]
            for s in range(6):
                t = stage_tile(s)
                jobs += [Job("kv", 1, t, gain=10), Job("kv", 1, NMT + t, gain=10), Job("in", 1, t, gain=4)]
            jobs += [Job("out", 1, m, kn=5, tag="early") for m in range(KT)]
            jobs += [Job("out", 1, m, k0=5, kn=3, halves=(h,), tag=h) for h in range(2) for m in range(KT)]
        g = 4 * l + 2
        jobs += [Job("ffn", l, (f, j), gain=g, halves=(h,), tag=h)
                 for h in range(2) for f in range(NHT) for j in range(2)]
        jobs += [Job("ffn", l, (f, j), gain=g) for f in range(NHT, CHUNKS[0]) for j in range(2)]
        for c, n in enumerate(CHUNKS):
            if c:
                jobs += [Job("ffn", l, (f, j), gain=g) for f in range(CH0[c], CH0[c] + n) for j in range(2)]
            if c < 2:
                jobs += [Job("down", l, (c, m), kn=n) for m in range(KT)]
            else:
                jobs += [Job("down", l, (c, m), kn=n, halves=(h,), tag=h)
                         for h in range(2) for m in range(KT)]
    return jobs


def stage_tile(s):
    return 2 * (s % 3) + s // 3


JOBS = plan_jobs()
NJ = len(JOBS)
J = {job.key: n for n, job in enumerate(JOBS)}

GAINED = [sum(1 for q in JOBS[:n + 1] if q.gain is not None) for n in range(NJ)]

READ_OUT = {}
_count = {}
for _n, _job in enumerate(JOBS):
    if _job.name == "mem":
        _s, _k = "mem_scaled", 1
    elif _job.name == "kv":
        _s, _k = ("swapped", 4) if _job.i < NMT else ("v_scaled", 1)
    elif _job.name == "in":
        _s, _k = ("q_scaled", 1) if _job.i >= NMT else (("in_scaled", 1) if _job.l == 0 else ("swapped", 4))
    elif _job.name == "pool":
        _s, _k = "ypool_done", 1
    elif _job.name == "out":
        _s, _k = ("y_first" if _job.l == 0 or _job.tag == "early" else "y_part"), 1
    elif _job.name == "ffn":
        _s, _k = ("up_scaled" if _job.i[1] else "silu_in"), 1
    else:
        _s, _k = ("y_part" if _job.i[0] else "y_first"), 1
    _count[_s] = _count.get(_s, 0) + _k
    READ_OUT[_n] = (_s, _count[_s])


def runs_of_jobs():
    runs = []
    for n, job in enumerate(JOBS):
        p = JOBS[n - 1] if n else None
        same = p and (p.name, p.l, p.k0, p.kn, p.gain) == (job.name, job.l, job.k0, job.kn, job.gain) \
            and job.row == p.row + 1
        if same:
            runs[-1][1] += 1
        else:
            runs.append([n, 1])
    return runs


RUNS = runs_of_jobs()


def build(nc, w_all, x_t, mem_t, pos, gains, consts, masks, out_t):
    with ExitStack() as ctx:
        base = nc.sbuf_base + (-nc.sbuf_base) % 64
        total = 222 * 1024
        ctx.enter_context(nc.sbuf_tensor("fence", [P, total // 4], F32))
        cursor = [base]

        def at(name, shape, dt, offset):
            return nc.alloc_sbuf_tensor_at(name, shape, dt, offset=offset)

        def take(nbytes):
            o = cursor[0]
            cursor[0] += nbytes + -nbytes % 32
            assert cursor[0] - base <= total
            return o

        def sem(name):
            return ctx.enter_context(nc.semaphore(name))

        TILE = 4 * S
        XH = at("XH", [P, KT, S], F32R, take(KT * TILE))
        XL = at("XL", [P, KT, S], F32R, take(KT * TILE))
        o_ch, o_cl = take(KT * TILE), take(KT * TILE)
        CH = at("CH", [P, KT, S], F32R, o_ch)
        CL = at("CL", [P, KT, S], F32R, o_cl)
        QF = at("QF", [P, KT, S], F32, o_ch)
        OF = at("OF", [P, KT, S], F32, o_cl)
        MR = at("MR", [P, KT, MEM], F32, o_ch + 6 * TILE)
        MS = at("MS", [P, KT, MEM], F32, o_cl + 6 * TILE)
        MV = at("MV", [P, 2, MEM], F32, o_cl + 4 * TILE)
        o_y = take(KT * TILE)
        Y = at("Y", [P, KT, S], F32, o_y)
        WR = at("WR", [P, 2, KT, P], F32, take(2 * TILE))
        WH = at("WH", [P, 2, KT, P], F32R, take(2 * TILE))
        WL = at("WL", [P, 2, KT, P], F32R, take(2 * TILE))
        RSTD = at("RSTD", [P, S], F32, take(TILE))
        SS = at("SS", [P, S], F32, take(TILE))
        TP = [at(f"TP{i}", [P, S + PAD], F32, take(4 * (S + PAD))) for i in range(4)]
        T = [t[:, PAD:PAD + S] for t in TP]
        KM = at("KM", [P, 2, MEM], F32, take(8 * MEM))
        VM = at("VM", [P, 4, P], F32, take(16 * P))
        SSM = at("SSM", [P, MEM], F32, take(4 * MEM))
        RSTDM = at("RSTDM", [P, MEM], F32, take(4 * MEM))
        GN = at("GN", [P, NGAIN], F32, take(4 * NGAIN))
        CN = at("CN", [P, NCONST], F32, take(4 * NCONST))
        MK = at("MK", [P, 3 * P], F32, take(12 * P))
        LX = at("LX", [P, 4, 2, DH], F32, take(4 * HT))
        MC = at("MC", [P, 2, 16], F32, take(128))
        LC = at("LC", [P, 2, 16], F32, take(128))
        LV = at("LV", [P, 16], F32, take(64))
        NM = at("NM", [P, 2], F32, take(32))
        RL = at("RL", [P, 2], F32, take(32))
        RC = at("RC", [P, 8], F32, take(32))
        COS = at("COS", [P, S], F32, o_y)
        SIN = at("SIN", [P, S], F32, o_y + TILE)
        POS = at("POS", [P, S], I32, o_y + TILE)
        KF = [at(f"KF{i}", [P, S], F32, o_y + (2 + 2 * i) * TILE) for i in range(2)]
        VF = [at(f"VF{i}", [P, 8, P], F32, o_y + (3 + 2 * i) * TILE) for i in range(2)]
        MX = at("MX", [P, S], F32, o_y + 6 * TILE)
        PR = at("PR", [P, 2, 256], F32, o_y + 7 * TILE)
        PT = at("PT", [P, 2, 256], F32, o_y + 7 * TILE + 2048)

        IDENT = CN[:, C_ID:C_ID + P]
        ONE = CN[:, C_ONE:C_ONE + 1]

        PS = [ctx.enter_context(nc.psum_tensor(f"PS{i}", [P, S], F32)) for i in range(2)]
        PSC = ctx.enter_context(nc.psum_tensor("PSC", [P, HT], F32))
        PTR = ctx.enter_context(nc.psum_tensor("PTR", [P, HT], F32))
        PO = ctx.enter_context(nc.psum_tensor("PO", [P, HT], F32))
        PX = ctx.enter_context(nc.psum_tensor("PX", [P, HT], F32))

        w_loaded = [sem(f"w_loaded{i}") for i in range(2)]
        w_gained = sem("w_gained")
        w_hi = sem("w_hi")
        w_lo = sem("w_lo")
        mm_done = sem("mm_done")
        consts_in, mem_in, pos_in = sem("consts_in"), sem("mem_in"), sem("pos_in")
        x_in = [[sem(f"x_in{h}_{k}") for k in range(KT)] for h in range(2)]
        out_done = sem("out_done")
        mem_sq, mem_hi = sem("mem_sq"), sem("mem_hi")
        mem_ss, mem_lo = sem("mem_ss"), sem("mem_lo")
        rc_done = sem("rc_done")
        px_full = sem("px_full")
        px_free = sem("px_free")
        sq_done = [sem(f"sq_done{i}") for i in range(2)]
        ss_done = [sem(f"ss_done{i}") for i in range(2)]
        x_sum = [sem(f"x_sum{i}") for i in range(2)]
        y_normed = [sem(f"y_normed{i}") for i in range(2)]
        res_done = [sem(f"res_done{i}") for i in range(2)]
        x_hi = [sem(f"x_hi{i}") for i in range(2)]
        x_lo = [sem(f"x_lo{i}") for i in range(2)]
        pads_zero = sem("pads_zero")
        pooled = sem("pooled")
        mix_ready = sem("mix_ready")
        c_hi, c_lo = sem("c_hi"), sem("c_lo")
        silu_done, prod_done = sem("silu_done"), sem("prod_done")
        a_hi, a_lo = sem("a_hi"), sem("a_lo")
        ang_ready, trig_done = sem("ang_ready"), sem("trig_done")
        cos_part = sem("cos_part")
        roped = sem("roped")
        scored = sem("scored")
        max_done = sem("max_done")
        exp_done = sem("exp_done")
        p_normed = sem("p_normed")
        p_tr = sem("p_tr")
        pt_done = sem("pt_done")
        pv_done = sem("pv_done")
        o_free = sem("o_free")
        ln_done, lv_done, lx_done = sem("ln_done"), sem("lv_done"), sem("lx_done")
        cmb_max = sem("cmb_max")
        cmb_diff = sem("cmb_diff")
        cmb_exp = sem("cmb_exp")
        cmb_sum = sem("cmb_sum")
        cmb_ln, cmb_inv = sem("cmb_ln"), sem("cmb_inv")
        cmb_part = sem("cmb_part")
        cmb_out = sem("cmb_out")
        dve_own, pool_own = sem("dve_own"), sem("pool_own")
        named = {"mem_scaled": sem("mem_scaled"), "swapped": sem("swapped"), "v_scaled": sem("v_scaled"),
                 "q_scaled": sem("q_scaled"), "in_scaled": sem("in_scaled"),
                 "ypool_done": sem("ypool_done"), "y_first": sem("y_first"), "y_part": sem("y_part"),
                 "up_scaled": sem("up_scaled"), "silu_in": sem("silu_in")}
        mem_scaled, swapped, v_scaled, q_scaled, in_scaled, ypool_done, y_first, y_part, up_scaled, \
            silu_in = named.values()

        def read_out(j):
            s, v = READ_OUT[j]
            return named[s], v

        SLOTS = [("mem", 0, 6), ("mem", 0, 7), ("mem", 1, 6), ("mem", 1, 7)]
        SLOTS += [("dil", 1, stage_tile(s)) for s in range(6)]
        A_END0, A_END = 32, 160

        def tile_of(a):
            sl, h, n = a // 16, (a // 8) % 2, a % 8
            kind, l, t = SLOTS[sl]
            if kind == "mem":
                return sl, kind, l, t, h, n, 0, MEM, None
            g = t // 2
            if g == 2:
                return sl, kind, l, t, h, n, P * n, P, (2 * P, 3 * P)
            if (g == 0 and n == 0) or (g == 1 and n % 2 == 0):
                return sl, kind, l, t, h, n, P * n, P, (P, 2 * P)
            return sl, kind, l, t, h, n, P * (n - 1), 2 * P, (0, 2 * P)

        def by_residue(ap, g):
            return ap.rearrange("p (l r) -> p r l", r=DIL[g])

        def natural_cols(ap, g, half):
            d = DIL[g]
            return by_residue(ap, g)[:, half * d // 2:(half + 1) * d // 2, :] if d > 1 else ap[:, HALF[half]]

        def bank_cols(ap, g):
            d = DIL[g]
            return ap.rearrange("p (r l) -> p r l", r=d // 2) if d > 1 else ap

        HOOKS = {}
        for m in range(NMT):
            HOOKS[J[("in", 0, m, None)]] = (1, 3, 5, 7)
        first_stage_job = J[("kv", 1, stage_tile(0), None)]
        counts = [7] * 6 + [5, 6, 6] + [5, 5, 6] * 3
        for n, c in enumerate(counts):
            HOOKS[first_stage_job + n] = tuple(range(KT - c, KT))
        for m in range(4):
            HOOKS[J[("out", 1, m, "early")]] = (0, 1, 2, 3, 4)

        PAIRS = [(f, (h,)) for h in range(2) for f in range(NHT)] + [(f, (0, 1)) for f in range(NHT, 22)]
        NP_ = len(PAIRS)

        def inner_ready(l, c, k):
            return NP_ * l + CH0[c] + k + NHT + 1

        def updates(l, h, m):
            if h == 0:
                return ()
            return RES_AT[m] if l == 0 else (m - 2,) if m >= 2 else ()

        def cols(halves):
            return HALF[halves[0]] if len(halves) == 1 else slice(0, S)

        px_order = {"PE": [], "ACT": []}
        att = {"PE": 0, "ACT": 0, "DVE": 0}
        block = ctx.enter_context(nc.Block())

        @block.tensor
        def _(pe):
            MM = nc.tensor.matmul

            def px_begin(key):
                n = len(px_order["PE"])
                if n:
                    pe.wait_ge(px_free, n)
                px_order["PE"].append(key)

            def job(j, rh, rl, hook=None, wait_k=None, ks=None, slot=None, free=None):
                o = JOBS[j] if isinstance(j, int) else None
                halves = o.halves if o else (0, 1)
                width = MEM if o and o.name == "mem" else None
                ks = ks if ks is not None else list(range(o.kn))
                slot = j % 2 if slot is None else slot
                pe.wait_ge(w_lo, j + 1)
                if free is None and j >= 2:
                    free = read_out(j - 2)
                if free is not None:
                    pe.wait_ge(*free)
                spans = [slice(0, width)] if width else [HALF[h] for h in halves]
                for i, k in enumerate(ks):
                    if wait_k is not None:
                        wait_k(k)
                    last = i == len(ks) - 1
                    for c in spans:
                        MM(PS[slot][:, c], WH[:, slot, i, :], rh(k)[:, c], start=(i == 0), stop=False)
                        MM(PS[slot][:, c], WH[:, slot, i, :], rl(k)[:, c], start=False, stop=False)
                    for c in spans:
                        ins = MM(PS[slot][:, c], WL[:, slot, i, :], rh(k)[:, c], start=False, stop=last)
                    if last:
                        ins.then_inc(mm_done, 1)
                    if hook is not None:
                        hook(i)

            xh, xl = (lambda k: XH[:, k, :]), (lambda k: XL[:, k, :])
            ch, cl = (lambda k: CH[:, k, :]), (lambda k: CL[:, k, :])

            def norm_columns(s, h):
                pe.wait_ge(ss_done[h], 8 * (s + 1))
                px_begin(("col", s, h))
                for t in range(4):
                    c = HT * h + P * t
                    ins = MM(PX[:, t:t + 1], SS[:, c:c + P], ONE, start=True, stop=True)
                ins.then_inc(px_full, 1)

            def norm_rows(s, h, count):
                pe.wait_ge(rc_done, count)
                px_begin(("row", s, h))
                for t in range(4):
                    ins = nc.tensor.transpose(PX[:, P * t:P * (t + 1)],
                                              RC[:, 4 * h + t:4 * h + t + 1].to_broadcast([P, P]), IDENT)
                ins.then_inc(px_full, 1)

            rc = [0]

            def norm(s, h):
                norm_columns(s, h)
                rc[0] += 1
                norm_rows(s, h, rc[0])

            def norm_hooks(places):
                def hook(i):
                    for part, s, h in places.get(i, ()):
                        if part == "col":
                            norm_columns(s, h)
                        else:
                            rc[0] += 1
                            norm_rows(s, h, rc[0])
                return hook

            def memory_columns(l):
                pe.wait_ge(mem_ss, l + 1)
                px_begin(("mcol", l))
                for t in range(2):
                    ins = MM(PX[:, t:t + 1], SSM[:, P * t:P * (t + 1)], ONE, start=True, stop=True)
                ins.then_inc(px_full, 1)

            def memory_rows(l):
                rc[0] += 1
                pe.wait_ge(rc_done, rc[0])
                px_begin(("mrow", l))
                for t in range(2):
                    ins = nc.tensor.transpose(PX[:, P * t:P * (t + 1)],
                                              RC[:, t:t + 1].to_broadcast([P, P]), IDENT)
                ins.then_inc(px_full, 1)

            def memory_products(l):
                pe.wait_ge(mem_lo, l + 1)
                mt = [c[:, 0:2, :].rearrange("p a (b t) -> p (a b) t", b=4) for c in (CH, CL)]
                for m in range(4):
                    job(J[("mem", l, m, None)], lambda k: mt[0][:, k, :], lambda k: mt[1][:, k, :])

            def memory_values(l):
                pe.wait_ge(mem_scaled, 4 * l + 4)
                px_begin(("mv", l))
                for t in range(2):
                    for m in range(2):
                        ins = nc.tensor.transpose(PX[:, (2 * t + m) * P:(2 * t + m + 1) * P],
                                                  MV[:, m, P * t:P * (t + 1)], IDENT)
                ins.then_inc(px_full, 1)

            def lse_rows(sl, r):
                pe.wait_ge(lx_done, 2 * (sl - 4) + r + 1)
                px_begin(("lse", sl, r))
                for n in range(4):
                    ins = nc.tensor.transpose(PX[:, P * n:P * (n + 1)],
                                              LX[:, n, :, :].rearrange("p h c -> p (h c)"), IDENT)
                ins.then_inc(px_full, 1)

            def step(_=None):
                a, end = att["PE"], A_END if att.get("second") else A_END0
                begin = 0 if end == A_END0 else A_END0
                att["PE"] += 1
                if begin <= a - 3 < end:
                    b = a - 3
                    sl, kind, l, t, h, n, k0, nk, _m = tile_of(b)
                    pe.wait_ge(pt_done, b + 1)
                    if b % 4 == 0 and b:
                        pe.wait_ge(o_free, b // 4)
                    for i in range(nk // P):
                        v = VM[:, 2 * i + t - NMT, :] if kind == "mem" else VF[sl % 2][:, k0 // P + i, :]
                        ins = MM(PO[:, P * (b % 4):P * (b % 4 + 1)], v, PT[:, b % 2, P * i:P * (i + 1)],
                                 start=(i == 0), stop=(i == nk // P - 1))
                    ins.then_inc(pv_done, 1)
                if begin <= a - 2 < end:
                    b = a - 2
                    nk = tile_of(b)[7]
                    pe.wait_ge(p_normed, b + 1)
                    if b:
                        pe.wait_ge(pt_done, b)
                    for i in range(nk // P):
                        ins = nc.tensor.transpose(PTR[:, P * i:P * (i + 1)], PR[:, b % 2, P * i:P * (i + 1)], IDENT)
                    ins.then_inc(p_tr, 1)
                if a < end:
                    sl, kind, l, t, h, n, k0, nk, _m = tile_of(a)
                    rows = slice(DH * h, DH * (h + 1))
                    if a % 16 == 0:
                        if kind == "mem":
                            pe.wait_ge(*read_out(J[("in", l, t, None if l == 0 else 1)]))
                            pe.wait_ge(mem_scaled, 4 * l + 4)
                            pe.wait_ge(px_free, px_order["PE"].index(("mv", l)) + 1)
                        else:
                            pe.wait_ge(roped, 2 * (sl - 4) + 2)
                            pe.wait_ge(px_free, px_order["PE"].index(("v", sl - 4, 1)) + 1)
                    keys = KM[rows, t - NMT, :] if kind == "mem" else KF[sl % 2][rows, k0:k0 + nk]
                    if a:
                        pe.wait_ge(exp_done, a)
                    MM(PSC[:, 0:nk], QF[rows, t, P * n:P * (n + 1)], keys,
                       start=True, stop=True).then_inc(scored, 1)
                if end == A_END and a >= 16 * 5 + 3 and (a - 3) % 16 in (0, 3):
                    sl, r = (a - 3) // 16 - 1, (a - 3) % 16 // 3
                    if sl >= 4:
                        lse_rows(sl, r)

            def steps_at(places):
                def hook(i):
                    if i in places:
                        step()
                return hook

            pe.wait_ge(consts_in, 32)
            memory_columns(0)
            memory_rows(0)
            memory_products(0)

            for n, m in enumerate((6, 7) + POOL_IN):
                j = J[("in", 0, m, None)]

                def x_ready(k):
                    for h in range(2):
                        pe.wait_ge(x_lo[h], k + 1)
                job(j, xh, xl, wait_k=x_ready if n == 0 else None,
                    hook=steps_at(HOOKS[j]) if m < NMT else
                    (lambda i: memory_values(0) if i == 2 else None) if n == 1 else None)
                if n == 0:
                    norm(0, 0)
                    norm(0, 1)
            for m in POOL_OUT:
                t, i = m // 3, m % 3
                ks = ((0, 1), (0, 1, 2), (1, 2))[i]
                pe.wait_ge(c_lo, 3 if t else 6)
                j = J[("pool", 0, m, None)]
                pe.wait_ge(w_lo, j + 1)
                pe.wait_ge(*read_out(j - 2))
                for q, k in enumerate(ks):
                    for c in HALF:
                        MM(PS[j % 2][:, c], WH[:, j % 2, k, :], CH[:, 3 * t + k, c], start=(q == 0), stop=False)
                        MM(PS[j % 2][:, c], WH[:, j % 2, k, :], CL[:, 3 * t + k, c], start=False, stop=False)
                    for c in HALF:
                        ins = MM(PS[j % 2][:, c], WL[:, j % 2, k, :], CH[:, 3 * t + k, c],
                                 start=False, stop=(q == len(ks) - 1))
                    if q == len(ks) - 1:
                        ins.then_inc(mm_done, 1)
                    if q in (0, len(ks) - 1):
                        step()
            while att["PE"] < A_END0 + 3:
                step()
            att["second"] = True
            att["PE"] = A_END0

            def sub_layer(l):
                s_y, s_x = 4 * l + 1, 4 * l + 2
                if l == 0:
                    for m in range(KT):
                        job(J[("out", 0, m, 0)], ch, cl, ks=OUT_ORDER[0],
                            wait_k=(lambda k: pe.wait_ge(c_lo, NMT + OUT_ORDER[0].index(k) + 1)) if m == 0 else None)
                    for m in range(KT):
                        job(J[("out", 0, m, 1)], ch, cl, ks=OUT_ORDER[0],
                            hook=norm_hooks({3: [("col", s_y, 0)], 6: [("row", s_y, 0)]}) if m == 0 else None)
                else:
                    for h in range(2):
                        for m in range(KT):
                            if m == 0 and h == 0:
                                pe.wait_ge(c_lo, 14 + 8)
                            job(J[("out", 1, m, h)], ch, cl, ks=OUT_ORDER[1][5:],
                                hook=norm_hooks({1: [("col", s_y, 0)]}) if h == 1 and m == 0 else
                                norm_hooks({0: [("row", s_y, 0)]}) if h == 1 and m == 1 else None)
                hooks = {(0, 0, 0): {7: [("col", s_x, 0)]},
                         (0, 0, 1): {2: [("row", s_x, 0), ("col", s_y, 1)], 5: [("row", s_y, 1)]},
                         (1, 0, 0): {7: [("col", s_x, 1)]},
                         (1, 0, 1): {3: [("row", s_x, 1)]}}
                for h in range(2):
                    for f in range(NHT):
                        for i in range(2):
                            places = hooks.get((h, f, i))
                            job(J[("ffn", l, (f, i), h)], xh, xl,
                                wait_k=(lambda k, h=h: pe.wait_ge(x_lo[h], 8 * (2 * l + 1) + k + 1))
                                if f == 0 and i == 0 else None,
                                hook=norm_hooks(places) if places else None)

                def inner_loop(f0, n, pair0):
                    j0 = J[("ffn", l, (f0, 0), None)]
                    for i in range(2):
                        job(j0 + i, xh, xl)
                    with pe.Fori(1, n) as it:
                        for i, s in enumerate((silu_in, up_scaled)):
                            job(2 * it + (j0 + i), xh, xl, ks=range(KT), slot=i, free=(s, it + pair0))

                inner_loop(NHT, CHUNKS[0] - NHT, NP_ * l + 2 * NHT)
                for c in range(3):
                    if c:
                        inner_loop(CH0[c], CHUNKS[c], NP_ * l + CH0[c] + NHT)
                    for m in range(KT):
                        if c < 2:
                            job(J[("down", l, (c, m), None)], ch, cl,
                                wait_k=(lambda k, c=c: pe.wait_ge(a_lo, inner_ready(l, c, k))) if m == 0 else None)
                        else:
                            job(J[("down", l, (c, m), 0)], ch, cl,
                                wait_k=(lambda k, c=c: pe.wait_ge(a_lo, inner_ready(l, c, k))) if m == 0 else None)
                for m in range(KT):
                    job(J[("down", l, (2, m), 1)], ch, cl,
                        hook=norm_hooks({2: [("col", 4 * l + 3, 0)], 5: [("row", 4 * l + 3, 0)]})
                        if m == 0 else None)

            sub_layer(0)

            def q_hook(i):
                norm_hooks({0: [("row", 4, 0), ("col", 3, 1)], 3: [("row", 3, 1)]})(i)
                if i == 5:
                    memory_columns(1)
                if i == 7:
                    memory_rows(1)

            for n, m in enumerate((6, 7)):
                job(J[("in", 1, m, 0)], xh, xl,
                    wait_k=(lambda k: pe.wait_ge(x_lo[0], 16 + k + 1)) if n == 0 else None,
                    hook=norm_hooks({7: [("col", 4, 0)]}) if n == 0 else q_hook)
            memory_products(1)
            for n, m in enumerate((6, 7)):
                job(J[("in", 1, m, 1)], xh, xl,
                    wait_k=(lambda k: pe.wait_ge(x_lo[1], 16 + k + 1)) if n == 0 else None,
                    hook=norm_hooks({3: [("col", 4, 1)], 6: [("row", 4, 1)]}) if n == 0 else
                    (lambda i: memory_values(1) if i == 2 else None))

            def v_rows(s, r):
                pe.wait_ge(v_scaled, s + 1)
                px_begin(("v", s, r))
                for n in range(4):
                    c = HT * r + P * n
                    ins = nc.tensor.transpose(PX[:, P * n:P * (n + 1)], T[3][:, c:c + P], IDENT)
                ins.then_inc(px_full, 1)

            for s in range(6):
                for i in range(3):
                    j = first_stage_job + 3 * s + i

                    def hook(k, places=HOOKS[j], i=i, s=s):
                        if k in places:
                            step()
                            q = places.index(k)
                            if i == 2 and q in (0, 3):
                                v_rows(s, q // 3)
                    job(j, xh, xl, hook=hook)
            for m in range(KT):
                j = J[("out", 1, m, "early")]
                if m == 0:
                    pe.wait_ge(c_lo, 12 + 2 + 2 + 3)
                job(j, ch, cl, ks=OUT_ORDER[1][0:5], hook=steps_at(HOOKS[j]) if j in HOOKS else
                    (lambda i: lse_rows(9, i // 2) if i in (0, 2) else None) if m == 4 else None)
                if m == 3:
                    while att["PE"] < A_END + 3:
                        step()
            sub_layer(1)
            norm(7, 1)

        @block.scalar
        def _(act):
            A = nc.scalar.activation

            def weight_hi(j, slot, kn, j_like=None):
                j_like = j if j_like is None else j_like
                if JOBS[j_like].gain is None:
                    act.wait_ge(w_loaded[slot], 16 * (j_like // 2 + 1))
                else:
                    act.wait_ge(w_gained, j + (GAINED[j_like] - j_like))
                if not isinstance(j, int) or j >= 2:
                    act.wait_ge(mm_done, j - 1)
                A(WH[:, slot, 0:kn, :], WR[:, slot, 0:kn, :], ACT.Copy).then_inc(w_hi, 1)

            def ahead(j):
                if j + 2 < NJ:
                    weight_hi(j + 2, j % 2, JOBS[j + 2].kn)

            def px_read(key, *ops):
                n = len(px_order["ACT"])
                px_order["ACT"].append(key)
                act.wait_ge(px_full, n + 1)
                for op in ops[:-1]:
                    op()
                ops[-1]().then_inc(px_free, 1)

            def norm_root(s, h):
                px_read(("col", s, h), lambda: A(RC[:, 4 * h:4 * h + 4], PX[:, 0:4], ACT.Sqrt, scale=1.0 / D,
                                                 bias=CN[:, C_EPS:C_EPS + 1]))

            def norm_row(s, h):
                px_read(("row", s, h), lambda: A(RSTD[:, HALF[h]], PX[:, :], ACT.Copy))

            def square(s, h, k, src):
                n = 8 * s + k
                if n >= 2:
                    act.wait_ge(ss_done[h], n - 1)
                A(T[2 + k % 2][:, HALF[h]], src, ACT.Square).then_inc(sq_done[h], 1)

            def residual(r, h, k):
                act.wait_ge(*((x_in[h][k], 16) if r == 0 else (res_done[h], 8 * (r - 1) + k + 1)))
                A(XH[:, k, HALF[h]], Y[:, k, HALF[h]], ACT.Copy).then_inc(x_hi[h], 1)
                square(2 * r, h, k, Y[:, k, HALF[h]])

            def memory_in(l):
                act.wait_ge(mem_in, 16 * (l + 1))
                A(MS[:, :, :], MR[:, :, :], ACT.Square).then_inc(mem_sq, 1)
                if l:
                    act.wait_ge(mm_done, J[("down", 0, (2, 7), 1)] + 1)
                A(CH[:, 0:2, :].rearrange("p a (b t) -> p (a b) t", b=4), MR[:, :, :],
                  ACT.Copy).then_inc(mem_hi, 1)

            def memory_root(l):
                px_read(("mcol", l), lambda: A(RC[:, 0:2], PX[:, 0:2], ACT.Sqrt, scale=1.0 / D,
                                               bias=CN[:, C_EPS:C_EPS + 1]))

            def memory_row(l):
                px_read(("mrow", l), lambda: A(RSTDM[:, :], PX[:, 0:MEM], ACT.Copy))

            def memory_values(l):
                px_read(("mv", l), lambda: A(VM[:, :, :].rearrange("p a b -> p (a b)"), PX[:, :], ACT.Copy))

            def step():
                a, end = att["ACT"], A_END if att.get("second_act") else A_END0
                begin = 0 if end == A_END0 else A_END0
                att["ACT"] += 1
                if begin <= a - 3 < end and (a - 3) % 4 == 3:
                    b = a - 3
                    sl, kind, l, t, h, n, _, _, _ = tile_of(b)
                    rows, half = slice(DH * h, DH * (h + 1)), n // 4
                    act.wait_ge(pv_done, b + 1)
                    if kind == "mem":
                        A(OF[rows, t, HALF[half]], PO[rows, :], ACT.Copy).then_inc(o_free, 1)
                    else:
                        g = t // 2
                        A(natural_cols(OF[rows, t, :], g, half), bank_cols(PO[rows, :], g),
                          ACT.Copy).then_inc(o_free, 1)
                if begin <= a - 2 < end:
                    b = a - 2
                    nk = tile_of(b)[7]
                    act.wait_ge(p_tr, b + 1)
                    if b >= 2:
                        act.wait_ge(pv_done, b - 1)
                    A(PT[:, b % 2, 0:nk], PTR[:, 0:nk], ACT.Copy).then_inc(pt_done, 1)
                if a < end:
                    sl, kind, l, t, h, n, k0, nk, mask = tile_of(a)
                    act.wait_ge(max_done, a + 1)
                    if a >= 2:
                        act.wait_ge(p_tr, a - 1)
                    A(PR[:, a % 2, 0:nk], PSC[:, 0:nk], ACT.Exp, scale=SCALE,
                      bias=NM[:, a % 2:a % 2 + 1],
                      accum_out=LC[:, sl % 2, 8 * h + n:8 * h + n + 1]).then_inc(exp_done, 1)
                if end == A_END and (a - 1) % 16 == 0 and a - 1 >= 16 * 5:
                    log_sums((a - 1) // 16 - 1)
                if end == A_END and a >= 16 * 5 + 4 and (a - 4) % 16 in (0, 3):
                    sl, r = (a - 4) // 16 - 1, (a - 4) % 16 // 3
                    lse_out(sl, r)

            def log_sums(sl):
                act.wait_ge(exp_done, 16 * (sl + 1))
                A(LV[:, :], LC[:, sl % 2, :], ACT.Ln).then_inc(ln_done, 1)

            def lse_out(sl, r):
                t = SLOTS[sl][2]
                g = t // 2
                px_read(("lse", sl, r), lambda: A(natural_cols(QF[:, t, :], g, r), bank_cols(PX[:, :], g),
                                                  ACT.Copy))

            act.wait_ge(consts_in, 32)
            memory_in(0)
            weight_hi(0, 0, KT)
            weight_hi(1, 1, KT)
            memory_root(0)
            memory_row(0)
            for k in range(KT):
                for h in range(2):
                    residual(0, h, k)
                if k < 4:
                    ahead(J[("mem", 0, k, None)])

            def split_pooled(n):
                act.wait_ge(mix_ready, n + 1)
                A(CH[:, POOL_IN[n], :], T[3], ACT.Copy).then_inc(c_hi, 1)

            for n, m in enumerate((6, 7) + POOL_IN):
                j = J[("in", 0, m, None)]
                for _ in HOOKS.get(j, ()):
                    step()
                if n >= 3:
                    split_pooled(n - 3)
                ahead(j)
                if n == 0:
                    norm_root(0, 0)
                    norm_row(0, 0)
                    norm_root(0, 1)
                    norm_row(0, 1)
                    memory_values(0)
            split_pooled(5)
            def split_product(n):
                act.wait_ge(ypool_done, n + 1)
                A(CH[:, POOL_OUT[n], :], Y[:, POOL_OUT[n], :], ACT.Copy).then_inc(c_hi, 1)

            for n, m in enumerate(POOL_OUT):
                j = J[("pool", 0, m, None)]
                step()
                step()
                act.wait_ge(mm_done, j + 1)
                A(Y[:, m, :], PS[j % 2][:, :], ACT.Copy,
                  scale=GN[:, G_POOL + m:G_POOL + m + 1]).then_inc(ypool_done, 1)
                ahead(j)
                if n >= 3:
                    split_product(n - 3)
            for n in range(3, NMT):
                split_product(n)
            while att["ACT"] < A_END0 + 3:
                step()
            att["second_act"] = True
            att["ACT"] = A_END0
            for m in range(2):
                act.wait_ge(o_free, 4 * (m + 1))
                A(CH[:, NMT + m, :], OF[:, NMT + m, :], ACT.Copy).then_inc(c_hi, 1)

            def first_y(s, j, m, halves):
                act.wait_ge(mm_done, j + 1)
                c = cols(halves)
                if s is not None:
                    square(s, halves[0], m, PS[j % 2][:, c])
                A(Y[:, m, c], PS[j % 2][:, c], ACT.Copy).then_inc(y_first, 1)

            def ffn_pair(l, pair, f_slot, c):
                act.wait_ge(silu_in, pair + 1)
                A(T[1][:, c], T[0][:, c], ACT.Silu).then_inc(silu_done, 1)

            def inner_hi(pair, dst, c):
                act.wait_ge(prod_done, pair + 1)
                A(dst, T[3][:, c], ACT.Copy).then_inc(a_hi, 1)

            def sub_layer(l):
                s_y, s_x = 4 * l + 1, 4 * l + 2
                for h in range(2):
                    for m in range(KT):
                        j = J[("out", l, m, h)]
                        if h == 1 and m == l:
                            norm_root(s_y, 0)
                            norm_row(s_y, 0)
                        if l == 0:
                            first_y(s_y, j, m, (h,))
                        else:
                            act.wait_ge(read_out(j)[0], read_out(j)[1])
                            square(s_y, h, m, Y[:, m, HALF[h]])
                        ahead(j)
                        for k in updates(l, h, m):
                            residual(2 * l + 1, 0, k)
                if l == 1:
                    residual(3, 0, 6)
                    residual(3, 0, 7)
                norm_root(s_x, 0)
                norm_row(s_x, 0)
                norm_root(s_y, 1)
                pair = NP_ * l
                for h in range(2):
                    for f in range(NHT):
                        j = J[("ffn", l, (f, 0), h)]
                        c = HALF[h]
                        ahead(j)
                        if f == 0:
                            norm_row(s_x if h else s_y, 1)
                        ffn_pair(l, pair, f, c)
                        if h == 0:
                            for k in RES_FFN[2 * f]:
                                residual(2 * l + 1, 1, k)
                        ahead(j + 1)
                        inner_hi(pair, CH[:, f, c], c)
                        if h == 0:
                            for k in RES_FFN[2 * f + 1]:
                                residual(2 * l + 1, 1, k)
                        pair += 1
                    if h == 0:
                        norm_root(s_x, 1)

                def inner_loop(f0, n, k0, pair0):
                    j0 = J[("ffn", l, (f0, 0), None)]
                    full = slice(0, S)
                    with act.Fori(0, n - 1) as it:
                        weight_hi(2 * it + (j0 + 2), 0, KT, j0 + 2)
                        ffn_pair(l, it + pair0, None, full)
                        weight_hi(2 * it + (j0 + 3), 1, KT, j0 + 3)
                        inner_hi(it + pair0, CH[:, bass.ds(it + k0, 1), :].rearrange("p a t -> p (a t)"), full)
                    last = j0 + 2 * (n - 1)
                    ahead(last)
                    ffn_pair(l, pair0 + n - 1, None, full)
                    ahead(last + 1)
                    inner_hi(pair0 + n - 1, CH[:, k0 + n - 1, :], full)

                inner_loop(NHT, CHUNKS[0] - NHT, NHT, NP_ * l + 2 * NHT)
                for c in range(3):
                    if c:
                        inner_loop(CH0[c], CHUNKS[c], 0, NP_ * l + CH0[c] + NHT)
                    if c < 2:
                        for m in range(KT):
                            j = J[("down", l, (c, m), None)]
                            if c == 0:
                                first_y(None, j, m, (0, 1))
                            ahead(j)
                    else:
                        for h in range(2):
                            for m in range(KT):
                                j = J[("down", l, (2, m), h)]
                                if h == 1 and m == 0:
                                    norm_root(4 * l + 3, 0)
                                    norm_row(4 * l + 3, 0)
                                act.wait_ge(*read_out(j))
                                square(4 * l + 3, h, m, Y[:, m, HALF[h]])
                                ahead(j)
                                if h == 1 and l == 0:
                                    for k in RES_AT[m]:
                                        residual(2, 0, k)

            sub_layer(0)

            memory_in(1)
            norm_root(4, 0)
            norm_row(4, 0)
            norm_root(3, 1)
            ahead(J[("in", 1, 6, 0)])
            norm_row(3, 1)
            memory_root(1)
            for k in range(4):
                residual(2, 1, k)
            memory_row(1)
            ahead(J[("in", 1, 7, 0)])
            for k in range(4, KT):
                residual(2, 1, k)
            for m in range(4):
                ahead(J[("mem", 1, m, None)])
            norm_root(4, 1)
            norm_row(4, 1)
            act.wait_ge(ang_ready, 1)
            A(SIN[:, :], T[0], ACT.Sin).then_inc(trig_done, 1)
            act.wait_ge(ang_ready, 2)
            A(COS[:, :], T[1], ACT.Sin, scale=-1.0, bias=CN[:, C_HPI:C_HPI + 1]).then_inc(trig_done, 1)
            ahead(J[("in", 1, 6, 1)])
            memory_values(1)
            ahead(J[("in", 1, 7, 1)])

            def swap_quarter(j, i):
                r, q = 32 * i, 32 * (i ^ 1)
                A(T[1][r:r + 32, :], PS[j % 2][q:q + 32, :], ACT.Copy).then_inc(swapped, 1)

            def combine(pair, stage):
                tiles = [2 * g + pair for g in range(3)]
                if stage == 0:
                    for g, t in enumerate(tiles):
                        act.wait_ge(cmb_diff, 3 * pair + g + 1)
                        A(QF[:, t, :], QF[:, t, :], ACT.Exp).then_inc(cmb_exp, 1)
                elif stage == 1:
                    tmp = MX[:, :] if pair == 0 else T[3]
                    act.wait_ge(cmb_sum, pair + 1)
                    A(tmp, tmp, ACT.Ln).then_inc(cmb_ln, 1)
                    act.wait_ge(cmb_ln, pair + 1)
                    A(tmp, tmp, ACT.Exp, scale=-1.0).then_inc(cmb_inv, 1)
                else:
                    for g, t in enumerate(tiles):
                        act.wait_ge(cmb_out, 3 * pair + g + 1)
                        A(CH[:, t, :], OF[:, t, :], ACT.Copy).then_inc(c_hi, 1)

            def split_memory():
                for m in range(2):
                    act.wait_ge(o_free, 8 + 4 * (m + 1))
                    A(CH[:, NMT + m, :], OF[:, NMT + m, :], ACT.Copy).then_inc(c_hi, 1)

            for n in range(19):
                j = first_stage_job + n
                prev = j - 1
                s, i = (n - 1) // 3, (n - 1) % 3
                todo = len(HOOKS[j]) if n < 18 else 0
                if n and i != 1:
                    act.wait_ge(cos_part, 2 * s + (1 if i == 0 else 2))
                for q in range(max(todo, 4)):
                    if q < todo:
                        step()
                    if n and i != 1 and q < 4:
                        swap_quarter(prev, q)
                    if n < 18 and n % 3 == 2 and q in (0, 3):
                        r = q // 3
                        ss = n // 3
                        px_v = lambda r=r, ss=ss: A(VF[ss % 2][:, 4 * r:4 * r + 4, :]
                                                    .rearrange("p a b -> p (a b)"), PX[:, :], ACT.Copy)
                        k = len(px_order["ACT"])
                        px_order["ACT"].append(("v", ss, r))
                        act.wait_ge(px_full, k + 1)
                        px_v().then_inc(px_free, 1)
                    if n and q == 1:
                        ahead(prev)
                if n == 8:
                    split_memory()
                if n == 15:
                    combine(0, 0)
                if n == 16:
                    combine(0, 1)
                if n == 17:
                    combine(0, 2)
            for m in range(KT):
                j = J[("out", 1, m, "early")]
                for _ in HOOKS.get(j, ()):
                    step()
                if m == 3:
                    while att["ACT"] < A_END + 3:
                        step()
                if m == 4:
                    lse_out(9, 0)
                    lse_out(9, 1)
                if 4 <= m < 7:
                    combine(1, m - 4)
                first_y(None, j, m, (0, 1))
                ahead(j)
            sub_layer(1)
            norm_root(7, 1)
            norm_row(7, 1)

        px_at = {key: n + 1 for n, key in enumerate(px_order["PE"])}
        assert px_order["PE"] == px_order["ACT"], [
            (n, x, y) for n, (x, y) in enumerate(zip(px_order["PE"], px_order["ACT"])) if x != y][:3]

        @block.vector
        def _(dve):
            V = nc.vector
            own = [0]
            rc = [0]

            def link(ins):
                own[0] += 1
                ins.then_inc(dve_own, 1)
                dve.wait_ge(dve_own, own[0])

            def weight_lo(j, slot, kn):
                dve.wait_ge(w_hi, j + 1)
                V.tensor_tensor(WL[:, slot, 0:kn, :], WR[:, slot, 0:kn, :], as_f32(WH[:, slot, 0:kn, :]),
                                ALU.subtract).then_inc(w_lo, 1)

            def ahead(j):
                if j + 2 < NJ:
                    weight_lo(j + 2, j % 2, JOBS[j + 2].kn)

            def invert(key, c, n):
                dve.wait_ge(px_free, px_at[key])
                rc[0] += 1
                V.reciprocal(RC[:, c:c + n], RC[:, c:c + n]).then_inc(rc_done, 1)

            def norm(s, h):
                invert(("col", s, h), 4 * h, 4)

            def residual(r, h, k):
                c = HALF[h]
                if k < KT and r > 0:
                    if k == 0:
                        dve.wait_ge(px_free, px_at[("row", 2 * r - 1, h)])
                    dve.wait_ge(sq_done[h], 8 * (2 * r - 1) + k + 1)
                    if r in (1,):
                        dve.wait_ge(y_first, READ_OUT[J[("out", 0, k, h)]][1])
                    V.tensor_tensor(Y[:, k, c], Y[:, k, c], RSTD[:, c], ALU.mult).then_inc(y_normed[h], 1)
                    dve.wait_ge(y_normed[h], 8 * (r - 1) + k + 1)
                    dve.wait_ge(x_sum[h], 8 * (r - 1) + k + 1)
                    gcol = 8 * (4 * ((r - 1) // 2) + (1 if r % 2 else 3)) + k
                    V.scalar_tensor_tensor(out=Y[:, k, c], in0=Y[:, k, c], scalar=GN[:, gcol:gcol + 1],
                                           in1=T[k % 2][:, c], op0=ALU.mult,
                                           op1=ALU.add).then_inc(res_done[h], 1)
                if k >= 1 and r < 4:
                    q = k - 1
                    dve.wait_ge(x_hi[h], 8 * r + q + 1)
                    V.tensor_tensor(XL[:, q, c], Y[:, q, c], as_f32(XH[:, q, c]),
                                    ALU.subtract).then_inc(x_lo[h], 1)

            def memory_in(l):
                dve.wait_ge(mem_sq, l + 1)
                V.tensor_reduce(SSM[:, :], MS[:, :, :].rearrange("p k t -> p t k"), AX_X,
                                ALU.add).then_inc(mem_ss, 1)
                dve.wait_ge(mem_hi, l + 1)
                V.tensor_tensor(CL[:, 0:2, :].rearrange("p a (b t) -> p (a b) t", b=4), MR[:, :, :],
                                as_f32(CH[:, 0:2, :].rearrange("p a (b t) -> p (a b) t", b=4)),
                                ALU.subtract).then_inc(mem_lo, 1)

            def memory_kv(l, m):
                j = J[("mem", l, m, None)]
                if m == 0:
                    dve.wait_ge(px_free, px_at[("mrow", l)])
                dve.wait_ge(mm_done, j + 1)
                if l and m == 0:
                    dve.wait_ge(scored, 32)
                V.tensor_tensor(KM[:, m, :] if m < 2 else MV[:, m - 2, :], PS[j % 2][:, 0:MEM],
                                RSTDM[:, :], ALU.mult).then_inc(mem_scaled, 1)
                ahead(j)

            def step():
                a, end = att["DVE"], A_END if att.get("second_dve") else A_END0
                begin = 0 if end == A_END0 else A_END0
                att["DVE"] += 1
                if a < end:
                    sl, kind, l, t, h, n, k0, nk, mask = tile_of(a)
                    dve.wait_ge(scored, a + 1)
                    if a >= 2:
                        dve.wait_ge(exp_done, a - 1)
                    mcol = MC[:, sl % 2, 8 * h + n:8 * h + n + 1]
                    score = PSC[:, 0:nk]
                    if kind == "mem":
                        link(V.tensor_reduce(mcol, score, AX_X, ALU.max))
                    else:
                        link(V.tensor_tensor_reduce(score, score, MK[:, mask[0]:mask[1]],
                                                    1.0, NEG, ALU.add, ALU.max, mcol))
                    V.tensor_scalar(NM[:, a % 2:a % 2 + 1], mcol, -SCALE, None, ALU.mult).then_inc(max_done, 1)
                if begin <= a - 1 < end:
                    b = a - 1
                    sl, _k, _l, _t, h, n, _k0, nk, _m = tile_of(b)
                    dve.wait_ge(exp_done, b + 1)
                    if b:
                        dve.wait_ge(p_normed, b)
                    link(V.reciprocal(RL[:, b % 2:b % 2 + 1], LC[:, sl % 2, 8 * h + n:8 * h + n + 1]))
                    V.tensor_scalar(PR[:, b % 2, 0:nk], PR[:, b % 2, 0:nk], RL[:, b % 2:b % 2 + 1], None,
                                    ALU.mult).then_inc(p_normed, 1)
                if end == A_END and a - 2 >= 16 * 5 and (a - 2) % 16 == 0:
                    log_sums((a - 2) // 16 - 1, 0)
                if end == A_END and a - 5 >= 16 * 5 and (a - 5) % 16 == 0:
                    log_sums((a - 5) // 16 - 1, 1)

            def log_sums(sl, r):
                if r == 0:
                    dve.wait_ge(ln_done, sl - 3)
                    V.scalar_tensor_tensor(out=LV[:, :], in0=MC[:, sl % 2, :], scalar=SCALE, in1=LV[:, :],
                                           op0=ALU.mult, op1=ALU.add).then_inc(lv_done, 1)
                    dve.wait_ge(lv_done, sl - 3)
                    if sl > 4:
                        dve.wait_ge(px_full, px_at[("lse", sl - 1, 1)])
                else:
                    dve.wait_ge(px_full, px_at[("lse", sl, 0)])
                V.tensor_copy(LX[:, :, :, :], LV[:, :].rearrange("p (h n) -> p n h", h=2)[:, 4 * r:4 * r + 4, :]
                              .unsqueeze(3).to_broadcast([P, 4, 2, DH])).then_inc(lx_done, 1)

            dve.wait_ge(consts_in, 32)
            memory_in(0)
            weight_lo(0, 0, KT)
            weight_lo(1, 1, KT)
            invert(("mcol", 0), 0, 2)
            for k in range(KT + 1):
                for h in range(2):
                    residual(0, h, k)
                if k < 4:
                    memory_kv(0, k)

            def pooled_tile(n):
                m = POOL_IN[n]
                levels = sum(w <= WINDOWS[(m * P + P - 1) // POOLG] for w in WINDOWS)
                dve.wait_ge(pooled, n + 1)
                V.scalar_tensor_tensor(out=T[3], in0=T[1 + (levels - 1) % 2],
                                       scalar=CN[:, C_INVW + m:C_INVW + m + 1], in1=T[0],
                                       op0=ALU.mult, op1=ALU.subtract).then_inc(mix_ready, 1)
                dve.wait_ge(c_hi, n + 1)
                V.tensor_tensor(CL[:, m, :], T[3], as_f32(CH[:, m, :]), ALU.subtract).then_inc(c_lo, 1)
                dve.wait_ge(c_lo, n + 1)

            for n, m in enumerate((6, 7) + POOL_IN):
                j = J[("in", 0, m, None)]
                for _ in HOOKS.get(j, ()):
                    step()
                if n >= 3:
                    pooled_tile(n - 3)
                if n == 0:
                    norm(0, 0)
                    norm(0, 1)
                    for h in range(2):
                        dve.wait_ge(px_free, px_at[("row", 0, h)])
                dve.wait_ge(mm_done, j + 1)
                if m < NMT:
                    if n == 2:
                        dve.wait_ge(pads_zero, 3)
                    V.tensor_tensor(T[0], PS[j % 2][:, :], RSTD[:, :], ALU.mult).then_inc(in_scaled, 1)
                else:
                    V.tensor_tensor(QF[:, m, :], PS[j % 2][:, :], RSTD[:, :], ALU.mult).then_inc(q_scaled, 1)
                ahead(j)
            pooled_tile(5)
            def split_product_low(n):
                m = POOL_OUT[n]
                dve.wait_ge(c_hi, NMT + n + 1)
                V.tensor_tensor(CL[:, m, :], Y[:, m, :], as_f32(CH[:, m, :]), ALU.subtract).then_inc(c_lo, 1)

            for n, m in enumerate(POOL_OUT):
                step()
                step()
                ahead(J[("pool", 0, m, None)])
                if n >= 3:
                    split_product_low(n - 3)
            for n in range(3, NMT):
                split_product_low(n)
            while att["DVE"] < A_END0 + 3:
                step()
            att["second_dve"] = True
            att["DVE"] = A_END0

            def split_low(t, n):
                dve.wait_ge(c_hi, n)
                V.tensor_tensor(CL[:, t, :], OF[:, t, :], as_f32(CH[:, t, :]), ALU.subtract).then_inc(c_lo, 1)

            for m in range(2):
                split_low(NMT + m, 2 * NMT + m + 1)

            def gate(j, slot, pair, c):
                dve.wait_ge(mm_done, j + 1)
                V.tensor_tensor(T[0][:, c], PS[slot][:, c], RSTD[:, c], ALU.mult).then_inc(silu_in, 1)

            def up(j, slot, pair, c):
                dve.wait_ge(mm_done, j + 1)
                V.tensor_tensor(T[2][:, c], PS[slot][:, c], RSTD[:, c], ALU.mult).then_inc(up_scaled, 1)
                dve.wait_ge(up_scaled, pair + 1)
                dve.wait_ge(silu_done, pair + 1)
                V.tensor_tensor(T[3][:, c], T[1][:, c], T[2][:, c], ALU.mult).then_inc(prod_done, 1)

            def inner_lo(pair, dst, hi, c):
                dve.wait_ge(a_hi, pair + 1)
                V.tensor_tensor(dst, T[3][:, c], as_f32(hi), ALU.subtract).then_inc(a_lo, 1)
                dve.wait_ge(a_lo, pair + 1)

            def add_y(j, m, halves):
                dve.wait_ge(mm_done, j + 1)
                c = cols(halves)
                V.tensor_tensor(Y[:, m, c], Y[:, m, c], PS[j % 2][:, c], ALU.add).then_inc(y_part, 1)

            def sub_layer(l):
                s_y, s_x = 4 * l + 1, 4 * l + 2
                for h in range(2):
                    for m in range(KT):
                        j = J[("out", l, m, h)]
                        if h == 1 and m == l:
                            norm(s_y, 0)
                        if l == 1:
                            if h == 0:
                                dve.wait_ge(y_first, READ_OUT[J[("out", 1, m, "early")]][1])
                            add_y(j, m, (h,))
                        ahead(j)
                        for k in updates(l, h, m):
                            residual(2 * l + 1, 0, k)
                if l == 1:
                    residual(3, 0, 6)
                    residual(3, 0, 7)
                residual(2 * l + 1, 0, KT)
                norm(s_x, 0)
                norm(s_y, 1)
                pair = NP_ * l
                for h in range(2):
                    for f in range(NHT):
                        j = J[("ffn", l, (f, 0), h)]
                        c = HALF[h]
                        ahead(j)
                        if f == 0:
                            dve.wait_ge(px_free, px_at[("row", s_x, h)])
                            dve.wait_ge(ss_done[h], 8 * (s_x + 1))
                        gate(j, 0, pair, c)
                        if h == 0:
                            for k in RES_FFN[2 * f]:
                                residual(2 * l + 1, 1, k)
                        up(j + 1, 1, pair, c)
                        ahead(j + 1)
                        inner_lo(pair, CL[:, f, c], CH[:, f, c], c)
                        if h == 0:
                            for k in RES_FFN[2 * f + 1]:
                                residual(2 * l + 1, 1, k)
                        pair += 1
                    if h == 0:
                        residual(2 * l + 1, 1, KT)
                        norm(s_x, 1)

                def inner_loop(f0, n, k0, pair0):
                    j0 = J[("ffn", l, (f0, 0), None)]
                    full = slice(0, S)
                    with dve.Fori(0, n - 1) as it:
                        gate(2 * it + j0, 0, it + pair0, full)
                        weight_lo(2 * it + (j0 + 2), 0, KT)
                        up(2 * it + (j0 + 1), 1, it + pair0, full)
                        weight_lo(2 * it + (j0 + 3), 1, KT)
                        inner_lo(it + pair0, CL[:, bass.ds(it + k0, 1), :].rearrange("p a t -> p (a t)"),
                                 CH[:, bass.ds(it + k0, 1), :].rearrange("p a t -> p (a t)"), full)
                    last = j0 + 2 * (n - 1)
                    gate(last, 0, pair0 + n - 1, full)
                    ahead(last)
                    up(last + 1, 1, pair0 + n - 1, full)
                    ahead(last + 1)
                    inner_lo(pair0 + n - 1, CL[:, k0 + n - 1, :], CH[:, k0 + n - 1, :], full)

                inner_loop(NHT, CHUNKS[0] - NHT, NHT, NP_ * l + 2 * NHT)
                for c in range(3):
                    if c:
                        inner_loop(CH0[c], CHUNKS[c], 0, NP_ * l + CH0[c] + NHT)
                    if c < 2:
                        for m in range(KT):
                            j = J[("down", l, (c, m), None)]
                            if c == 1:
                                dve.wait_ge(y_first, READ_OUT[J[("down", l, (0, m), None)]][1])
                                add_y(j, m, (0, 1))
                            ahead(j)
                    else:
                        for h in range(2):
                            for m in range(KT):
                                j = J[("down", l, (2, m), h)]
                                if h == 1 and m == 0:
                                    norm(4 * l + 3, 0)
                                dve.wait_ge(y_part, READ_OUT[J[("down", l, (1, m), None)]][1])
                                add_y(j, m, (h,))
                                ahead(j)
                                if h == 1:
                                    for k in RES_AT[m]:
                                        residual(2 * l + 2, 0, k)

            sub_layer(0)
            residual(2, 0, KT)

            memory_in(1)
            dve.wait_ge(mem_lo, 2)
            norm(4, 0)
            norm(3, 1)
            for n, m in enumerate((6, 7)):
                j = J[("in", 1, m, 0)]
                dve.wait_ge(mm_done, j + 1)
                if n == 0:
                    dve.wait_ge(px_free, px_at[("row", 4, 0)])
                V.tensor_tensor(QF[:, m, HALF[0]], PS[j % 2][:, HALF[0]], RSTD[:, HALF[0]],
                                ALU.mult).then_inc(q_scaled, 1)
                ahead(j)
                for k in range(4 * n, 4 * n + 4):
                    residual(2, 1, k)
                    if k == 1:
                        invert(("mcol", 1), 0, 2)
            residual(2, 1, KT)
            two_pi = 2.0 * np.pi
            c1 = 6.28125
            c2 = float(np.round((two_pi - c1) * 2 ** 21) / 2 ** 21)
            c3 = float(np.float32(two_pi - c1 - c2))
            pi_below = 3.1415925
            memory_kv(1, 0)
            dve.wait_ge(pos_in, 32)
            link(V.tensor_copy(T[0], POS[:, :]))
            link(V.tensor_scalar(T[0], T[0], CN[:, C_FREQ:C_FREQ + 1], None, ALU.mult))
            memory_kv(1, 1)
            link(V.tensor_scalar(T[1], T[0], float(1.0 / two_pi), ROUND, ALU.mult, ALU.add))
            link(V.tensor_scalar(T[1], T[1], ROUND, None, ALU.subtract))
            memory_kv(1, 2)
            for part in (c1, c2, c3):
                link(V.scalar_tensor_tensor(out=T[0], in0=T[1], scalar=-part, in1=T[0],
                                            op0=ALU.mult, op1=ALU.add))
            memory_kv(1, 3)
            link(V.tensor_scalar(T[0], T[0], pi_below, -pi_below, ALU.min, ALU.max))
            V.tensor_scalar(T[1], T[0], -1.0, None, ALU.mult).then_inc(ang_ready, 1)
            dve.wait_ge(ang_ready, 1)
            V.tensor_tensor(T[1], T[1], T[0], ALU.max).then_inc(ang_ready, 1)
            norm(4, 1)
            dve.wait_ge(px_free, px_at[("row", 4, 1)])
            for n, m in enumerate((6, 7)):
                j = J[("in", 1, m, 1)]
                dve.wait_ge(mm_done, j + 1)
                V.tensor_tensor(QF[:, m, HALF[1]], PS[j % 2][:, HALF[1]], RSTD[:, HALF[1]],
                                ALU.mult).then_inc(q_scaled, 1)
                ahead(j)
            dve.wait_ge(trig_done, 2)
            link(V.scalar_tensor_tensor(out=SIN[:, :], in0=SIN[:, :], scalar=CN[:, C_SIGN:C_SIGN + 1],
                                        in1=RSTD[:, :], op0=ALU.mult, op1=ALU.mult))
            link(V.tensor_tensor(COS[:, :], COS[:, :], RSTD[:, :], ALU.mult))

            def rotate(n, dst, g):
                dve.wait_ge(swapped, 4 * (n + 1))
                link(V.tensor_tensor(T[1], T[1], SIN[:, :], ALU.mult))
                dve.wait_ge(cos_part, n + 1)
                if DIL[g] > 1:
                    V.tensor_tensor(dst.rearrange("p (r l) -> p r l", r=DIL[g]), by_residue(T[0], g),
                                    by_residue(T[1], g), ALU.add).then_inc(roped, 1)
                else:
                    V.tensor_tensor(dst, T[0], T[1], ALU.add).then_inc(roped, 1)
                dve.wait_ge(roped, n + 1)

            def group_max(pair):
                tmp = MX[:, :] if pair == 0 else T[3]
                tiles = [2 * g + pair for g in range(3)]
                dve.wait_ge(px_free, px_at[("lse", 6 + 3 * pair, 1)])
                if pair:
                    dve.wait_ge(px_full, px_at[("v", 5, 1)])
                V.tensor_tensor(tmp, QF[:, tiles[0], :], QF[:, tiles[1], :], ALU.max).then_inc(cmb_max, 1)
                dve.wait_ge(cmb_max, 2 * pair + 1)
                V.tensor_tensor(tmp, tmp, QF[:, tiles[2], :], ALU.max).then_inc(cmb_max, 1)

            def combine_last(part):
                tiles = [2 * g + 1 for g in range(3)]
                if part == 0:
                    group_max(1)
                    dve.wait_ge(cmb_max, 4)
                    for t in tiles:
                        V.tensor_tensor(QF[:, t, :], QF[:, t, :], T[3], ALU.subtract).then_inc(cmb_diff, 1)
                elif part == 1:
                    dve.wait_ge(cmb_diff, 6)
                    dve.wait_ge(cmb_exp, 5)
                    link(V.tensor_tensor(T[3], QF[:, tiles[0], :], QF[:, tiles[1], :], ALU.add))
                    dve.wait_ge(cmb_exp, 6)
                    V.tensor_tensor(T[3], T[3], QF[:, tiles[2], :], ALU.add).then_inc(cmb_sum, 1)
                    dve.wait_ge(o_free, 40)
                    for t in tiles:
                        V.tensor_tensor(OF[:, t, :], OF[:, t, :], QF[:, t, :], ALU.mult).then_inc(cmb_part, 1)
                else:
                    dve.wait_ge(cmb_inv, 2)
                    for n, t in enumerate(tiles):
                        dve.wait_ge(cmb_part, 3 + n + 1)
                        V.tensor_tensor(OF[:, t, :], OF[:, t, :], T[3], ALU.mult).then_inc(cmb_out, 1)
                    for n, t in enumerate(tiles):
                        split_low(t, 19 + n + 1)

            for n in range(19):
                j = first_stage_job + n
                prev = j - 1
                s, i = (n - 1) // 3, (n - 1) % 3
                t = stage_tile(s) if n else 0
                g = t // 2
                todo = len(HOOKS[j]) if n < 18 else 0
                if n:
                    dve.wait_ge(mm_done, prev + 1)
                    if i != 1:
                        V.tensor_tensor(T[0], PS[prev % 2][:, :], COS[:, :], ALU.mult).then_inc(cos_part, 1)
                    else:
                        if s:
                            dve.wait_ge(px_full, px_at[("v", s - 1, 1)])
                        if DIL[g] > 1:
                            V.tensor_tensor(T[3].rearrange("p (r l) -> p r l", r=DIL[g]),
                                            by_residue(PS[prev % 2][:, :], g), by_residue(RSTD[:, :], g),
                                            ALU.mult).then_inc(v_scaled, 1)
                        else:
                            V.tensor_tensor(T[3], PS[prev % 2][:, :], RSTD[:, :],
                                            ALU.mult).then_inc(v_scaled, 1)
                for q in range(max(todo, 5 if n == 18 else 0)):
                    if q < todo:
                        step()
                    if n and i != 1 and q == 4:
                        rotate(2 * s + (0 if i == 0 else 1), KF[s % 2][:, :] if i == 0 else QF[:, t, :], g)
                    if n and q == 1:
                        ahead(prev)
                if n == 14:
                    group_max(0)
                if n == 8:
                    for m in range(2):
                        split_low(NMT + m, 14 + m + 1)
                if n == 17:
                    for g_ in range(3):
                        split_low(2 * g_, 16 + g_ + 1)
            for m in range(KT):
                j = J[("out", 1, m, "early")]
                for _ in HOOKS.get(j, ()):
                    step()
                if m == 3:
                    while att["DVE"] < A_END + 3:
                        step()
                    log_sums(9, 1)
                if 4 <= m < 7:
                    combine_last(m - 4)
                ahead(j)
            sub_layer(1)
            norm(7, 1)
            for k in range(KT):
                residual(4, 1, k)

        @block.gpsimd
        def _(pool):
            G = nc.gpsimd
            own = [0]
            gained = [0]

            def link(ins):
                own[0] += 1
                ins.then_inc(pool_own, 1)
                pool.wait_ge(pool_own, own[0])

            def gain(j, slot, loads, kn, k0, g):
                pool.wait_ge(w_loaded[slot], 16 * loads)
                raw = WR[:, slot, 0:kn, :]
                G.tensor_tensor(raw, raw, GN[:, 8 * g:8 * g + kn].unsqueeze(2).to_broadcast([P, kn, P]),
                                ALU.mult).then_inc(w_gained, 1)

            def gains_to(end):
                end = min(end, NJ)
                while gained[0] < end:
                    a = gained[0]
                    o = JOBS[a]
                    b = a
                    while b < end and (JOBS[b].kn, JOBS[b].gain) == (o.kn, o.gain):
                        b += 1
                    if o.gain is None:
                        gained[0] = b
                    elif b - a >= 4 and a % 2 == 0:
                        pairs = (b - a) // 2
                        with pool.Fori(0, pairs) as it:
                            for i in range(2):
                                gain(a + i + 2 * it, i, it + (a // 2 + 1), o.kn, o.k0, o.gain)
                        gained[0] = a + 2 * pairs
                    else:
                        gain(a, a % 2, a // 2 + 1, o.kn, o.k0, o.gain)
                        gained[0] = a + 1

            def accumulate(s, h, k):
                pool.wait_ge(sq_done[h], 8 * s + k + 1)
                src, dst = T[2 + k % 2][:, HALF[h]], SS[:, HALF[h]]
                if k == 0:
                    if s:
                        pool.wait_ge(px_full, px_at[("col", s - 1, h)])
                    G.tensor_copy(dst, src).then_inc(ss_done[h], 1)
                else:
                    pool.wait_ge(ss_done[h], 8 * s + k)
                    G.tensor_tensor(dst, dst, src, ALU.add).then_inc(ss_done[h], 1)

            def stream_sum(r, h, k):
                if k >= 2:
                    pool.wait_ge(res_done[h], 8 * (r - 1) + k - 1)
                elif r == 1:
                    pool.wait_ge(c_lo, 6)
                elif r in (2, 4):
                    pool.wait_ge(a_lo, NP_ * (r // 2))
                elif r == 3:
                    pool.wait_ge(roped, 12)
                G.tensor_tensor(T[k % 2][:, HALF[h]], as_f32(XH[:, k, HALF[h]]), as_f32(XL[:, k, HALF[h]]),
                                ALU.add).then_inc(x_sum[h], 1)

            pool.wait_ge(consts_in, 32)
            for i in range(3):
                G.memset(TP[i][:, 0:PAD], 0.0).then_inc(pads_zero, 1)
            gains_to(4)
            for k in range(KT):
                for h in range(2):
                    accumulate(0, h, k)
                if k < 4:
                    gains_to(5 + k)

            first = J[("in", 0, POOL_IN[0], None)]
            gains_to(first + 3)
            pool.wait_ge(pads_zero, 3)
            for n, m in enumerate(POOL_IN):
                pool.wait_ge(in_scaled, n + 1)
                if n:
                    pool.wait_ge(mix_ready, n)
                levels = []
                for w in WINDOWS:
                    rows = [r for r in range(P) if WINDOWS[(m * P + r) // POOLG] >= w]
                    if rows:
                        levels.append((w // 2, rows[0]))
                src = TP[0]
                for i, (shift, r0) in enumerate(levels):
                    dst = TP[1 + i % 2]
                    if r0:
                        link(G.tensor_copy(dst[0:r0, PAD:], src[0:r0, PAD:]))
                    link(G.tensor_tensor(dst[r0:P, PAD:], src[r0:P, PAD:],
                                         src[r0:P, PAD - shift:PAD + S - shift], ALU.add))
                    src = dst
                edge = CN[:, C_EDGE + PAD * m:C_EDGE + PAD * (m + 1)]
                G.tensor_tensor(src[:, PAD:2 * PAD], src[:, PAD:2 * PAD], edge, ALU.mult).then_inc(pooled, 1)
                gains_to(first + n + 4)

            def sub_layer(l):
                s_y, s_x = 4 * l + 1, 4 * l + 2
                j_out = J[("out", l, 0, 0)]
                lag = 0 if l == 0 else 2
                for m in range(KT):
                    accumulate(s_y, 0, m)
                stream_sum(2 * l + 1, 0, 0)
                stream_sum(2 * l + 1, 0, 1)
                for m in range(KT + lag):
                    if m < KT:
                        accumulate(s_y, 1, m)
                        gains_to(j_out + KT + m + 4)
                    for k in updates(l, 1, m):
                        accumulate(s_x, 0, k)
                        if k + 2 < KT:
                            stream_sum(2 * l + 1, 0, k + 2)
                j_ffn = J[("ffn", l, (0, 0), 0)]
                stream_sum(2 * l + 1, 1, 0)
                stream_sum(2 * l + 1, 1, 1)
                for k in range(KT):
                    gains_to(j_ffn + k + 4)
                    accumulate(s_x, 1, k)
                    if k + 2 < KT:
                        stream_sum(2 * l + 1, 1, k + 2)
                j_down = J[("down", l, (2, 0), 0)]
                gains_to(j_down)
                for m in range(KT):
                    accumulate(4 * l + 3, 0, m)
                stream_sum(2 * l + 2, 0, 0)
                stream_sum(2 * l + 2, 0, 1)
                for m in range(KT):
                    accumulate(4 * l + 3, 1, m)
                    gains_to(j_down + KT + m + 4)
                    for k in RES_AT[m]:
                        if l == 0:
                            accumulate(4, 0, k)
                        if k + 2 < KT:
                            stream_sum(2 * l + 2, 0, k + 2)

            sub_layer(0)
            stream_sum(2, 1, 0)
            stream_sum(2, 1, 1)
            j_in = J[("in", 1, 6, 0)]
            for k in range(KT):
                if k == 0:
                    gains_to(j_in + 4)
                if k == 4:
                    gains_to(j_in + 5)
                accumulate(4, 1, k)
                if k + 2 < KT:
                    stream_sum(2, 1, k + 2)

            def combine(part):
                tiles = [2 * g for g in range(3)]
                if part == 0:
                    pool.wait_ge(cmb_max, 2)
                    for t in tiles:
                        G.tensor_tensor(QF[:, t, :], QF[:, t, :], MX[:, :], ALU.subtract).then_inc(cmb_diff, 1)
                elif part == 1:
                    pool.wait_ge(cmb_diff, 3)
                    pool.wait_ge(cmb_exp, 3)
                    link(G.tensor_tensor(MX[:, :], QF[:, tiles[0], :], QF[:, tiles[1], :], ALU.add))
                    G.tensor_tensor(MX[:, :], MX[:, :], QF[:, tiles[2], :], ALU.add).then_inc(cmb_sum, 1)
                    pool.wait_ge(o_free, 28)
                    for t in tiles:
                        G.tensor_tensor(OF[:, t, :], OF[:, t, :], QF[:, t, :], ALU.mult).then_inc(cmb_part, 1)
                else:
                    pool.wait_ge(cmb_inv, 1)
                    for n, t in enumerate(tiles):
                        pool.wait_ge(cmb_part, n + 1)
                        G.tensor_tensor(OF[:, t, :], OF[:, t, :], MX[:, :], ALU.mult).then_inc(cmb_out, 1)

            gains_to(first_stage_job + 17)
            combine(0)
            gains_to(first_stage_job + 18)
            combine(1)
            combine(2)
            sub_layer(1)
            stream_sum(4, 1, 0)
            stream_sum(4, 1, 1)
            for k in range(2, KT):
                stream_sum(4, 1, k)

        @block.sync
        def _(sp):
            loaded = [0]

            def load(j, slot, row, o):
                if not isinstance(j, int) or j >= 2:
                    sp.wait_ge(w_lo, j - 1)
                sp.dma_start(WR[:, slot, 0:o.kn, :],
                             w_all[bass.ds(row, 1), :, o.k0 * P:(o.k0 + o.kn) * P]
                             .rearrange("a p (k n) -> (a p) k n", k=o.kn)).then_inc(w_loaded[slot], 16)

            def loads_to(end):
                for a, n in RUNS:
                    a, b = max(a, loaded[0]), min(a + n, end)
                    if b - a >= 6 and a % 2 == 0:
                        pairs = (b - a) // 2
                        with sp.Fori(0, pairs) as it:
                            for i in range(2):
                                load(a + i + 2 * it, i, JOBS[a].row + i + 2 * it, JOBS[a])
                        a += 2 * pairs
                    for j in range(a, b):
                        load(j, j % 2, JOBS[j].row, JOBS[j])
                loaded[0] = max(loaded[0], end)

            sp.dma_start(MR[:, :, :], mem_t).then_inc(mem_in, 16)
            sp.dma_start(CN[:, :], consts).then_inc(consts_in, 16)
            sp.dma_start(GN[:, :], gains).then_inc(consts_in, 16)
            loads_to(2)
            for k in range(KT):
                if k == 3:
                    loads_to(4)
                for h in range(2):
                    sp.dma_start(Y[:, k, HALF[h]], x_t[:, k, HALF[h]]).then_inc(x_in[h][k], 16)
            sp.dma_start(MK[:, :], masks).then_inc(pos_in, 16)
            loads_to(J[("in", 1, 6, 0)])
            sp.wait_ge(mm_done, J[("down", 0, (1, 7), None)] + 1)
            sp.dma_start(MR[:, :, :], mem_t).then_inc(mem_in, 16)
            loads_to(first_stage_job - 2)
            for h in range(2):
                sp.wait_ge(x_lo[h], 24)
                sp.wait_ge(sq_done[h], 8 * 5)
            sp.dma_start(POS[:, :], pos.to_broadcast([P, S])).then_inc(pos_in, 16)
            loads_to(NJ)
            for h in range(2):
                for k in range(KT):
                    sp.wait_ge(res_done[h], 8 * 3 + k + 1)
                    sp.dma_start(out_t[:, k, HALF[h]], Y[:, k, HALF[h]]).then_inc(out_done, 16)
            sp.wait_ge(out_done, 16 * 2 * KT)


def pack_weights(inp):
    w_all = np.zeros((len(ROWS), P, KT * P), np.float32)
    pool = np.zeros((2, 3 * P, 3 * P), np.float32)
    for g in range(4):
        r = (g % 2) * POOLG
        pool[g // 2, r:r + POOLG, r:r + POOLG] = inp["w_pool"][0, g]
    for n, (name, l, i) in enumerate(ROWS):
        if name == "mem":
            w = inp["w_mem_kv"][l][:, P * i:P * (i + 1)]
        elif name == "kv":
            w = inp["w_kv"][:, P * i:P * (i + 1)]
        elif name == "in":
            w = inp["w_in"][l][:, P * i:P * (i + 1)]
        elif name == "pool":
            w = pool[i // 3][:, P * (i % 3):P * (i % 3 + 1)]
        elif name == "out":
            w = inp["w_out"][l][:, P * i:P * (i + 1)]
            w = w.reshape(KT, P, P)[list(OUT_ORDER[l])].reshape(D, P)
        elif name == "ffn":
            f, j = i
            w = inp["w_gate_up"][l][:, j * DFF + P * f:j * DFF + P * (f + 1)]
        else:
            c, m = i
            w = inp["w_down"][l][P * CH0[c]:P * (CH0[c] + CHUNKS[c]), P * m:P * (m + 1)]
        k = w.shape[0] // P
        w_all[n, :, 0:k * P] = w.reshape(k, P, P).transpose(1, 0, 2).reshape(P, k * P)
    return w_all


def constant_tables():
    c = np.zeros((P, NCONST), np.float32)
    c[:, C_ID:C_ID + P] = np.eye(P)
    c[:, C_ONE:C_ONE + 8] = 1.0
    p = np.arange(P)
    for m in range(NMT):
        w = np.array(WINDOWS)[(m * P + p) // POOLG]
        c[:, C_INVW + m] = 1.0 / w
        for t in range(PAD):
            c[:, C_EDGE + PAD * m + t] = w / np.minimum(t + 1, w)
    half = DH // 2
    freqs = np.float32(10000.0) ** (-np.arange(half, dtype=np.float32) / half)
    c[:, C_FREQ] = freqs[p % half]
    c[:, C_SIGN] = np.where(p % DH < half, -1.0, 1.0)
    c[:, C_EPS] = EPS
    c[:, C_HPI] = np.pi / 2
    q, k = np.meshgrid(p, p, indexing="ij")
    prev = np.where(k >= q, 0.0, NEG)
    causal = np.where(k <= q, 0.0, NEG)
    by_residue = np.where((k <= q) & (k // 64 == q // 64), 0.0, NEG)
    return c, np.concatenate([prev, causal, by_residue], 1).astype(np.float32)


def kernel(**inputs):
    import concourse.bacc as bacc
    from concourse.bass_utils import run_bass_kernel_spmd

    inp = {k: np.asarray(v) for k, v in inputs.items()}
    tiles = lambda a: np.ascontiguousarray(a.T.reshape(KT, P, -1).transpose(1, 0, 2))
    columns = lambda a: a.reshape(-1, P).T
    consts, masks = constant_tables()
    gains = np.concatenate([columns(inp["norm_gains"]), columns(inp["mem_norm"]), columns(inp["kv_norm"]),
                            columns(inp["pool_scale"])], 1)
    arrays = {
        "in_w": pack_weights(inp),
        "in_x": tiles(inp["x"][0]),
        "in_mem": tiles(inp["mem"][0]),
        "in_pos": np.ascontiguousarray(inp["positions"]),
        "in_gains": np.ascontiguousarray(gains),
        "in_consts": consts,
        "in_masks": masks,
    }
    nc = bacc.Bacc("TRN2", target_bir_lowering=False, num_devices=1, dynamic_dma_scratch_size=1024)
    aps = [nc.dram_tensor(n, a.shape, mybir.dt.from_np(a.dtype), kind="ExternalInput").ap()
           for n, a in arrays.items()]
    out_t = nc.dram_tensor("out_t", (P, KT, S), F32, kind="ExternalOutput").ap()
    build(nc, *aps, out_t)
    got = run_bass_kernel_spmd(nc, [arrays], core_ids=[0]).results[0]["out_t"]
    return np.ascontiguousarray(got.transpose(1, 0, 2).reshape(D, S).T)[None]
```
